# Optimizing a Trainium2 kernel written in Bass

```python
import math
import jax, jax.numpy as jnp
from jax import lax
import numpy as np

D_MODEL = 1024
BATCH = 1
SEQ = 1024
DEPTH = 1

N_MEM = 256
HEAD_DIM = 64
N_DIL_HEADS = 8
N_FOX_HEADS = 8
DIL_WIDTH = N_DIL_HEADS * HEAD_DIM
FOX_WIDTH = N_FOX_HEADS * HEAD_DIM
MIX_WIDTH = DIL_WIDTH + FOX_WIDTH
IN_WIDTH = 3 * DIL_WIDTH + 3 * FOX_WIDTH + N_FOX_HEADS
DIL_CONFIGS = ((128, 1), (512, 4), (2048, 16))
BLOCK = 128
N_XATTN_HEADS = 4
XATTN_HEAD_DIM = D_MODEL // N_XATTN_HEADS
D_FF = 4 * D_MODEL
EPS = 1e-6
NEG = -1e30

kernel_name = "hybrid_dilated_fox_block"

def _rmsnorm(x, g):
    x32 = x.astype(jnp.float32)
    y = x32 * lax.rsqrt(jnp.mean(x32 * x32, axis=-1, keepdims=True) + EPS) * g.astype(jnp.float32)
    return y.astype(x.dtype)

def _alibi_slopes(n):
    return 2.0 ** (-(jnp.arange(1, n + 1, dtype=jnp.float32) * (8.0 / n)))

def _dilated_branch(q, k, v, slopes, window, dilation):
    B, S, H, Dh = q.shape
    span = dilation * BLOCK
    s_pad = -(-S // span) * span
    pad = ((0, 0), (0, s_pad - S), (0, 0), (0, 0))
    q, k, v = (jnp.pad(a, pad) for a in (q, k, v))
    L = s_pad // dilation
    nb = L // BLOCK

    def to_res(a):
        return a.reshape(B, L, dilation, H, Dh).transpose(0, 2, 1, 3, 4).reshape(B, dilation, nb, BLOCK, H, Dh)

    def with_prev(a):
        prev = jnp.pad(a, ((0, 0), (0, 0), (1, 0), (0, 0), (0, 0), (0, 0)))[:, :, :-1]
        return jnp.concatenate([prev, a], axis=3)

    qr = to_res(q)
    kb = with_prev(to_res(k))
    vb = with_prev(to_res(v))

    steps = window // dilation
    qi = jnp.arange(BLOCK)[:, None]
    kj = jnp.arange(2 * BLOCK)[None, :]
    delta = qi + BLOCK - kj
    blk = jnp.arange(nb)[:, None, None]
    valid = (delta >= 0) & (delta <= steps) & ((blk > 0) | (kj >= BLOCK))
    dist = (delta * dilation).astype(jnp.float32)
    bias = jnp.where(valid[:, None], -slopes[None, :, None, None] * dist[None, None], NEG)

    scale = 1.0 / math.sqrt(Dh)
    s = jnp.einsum('brnqhd,brnkhd->brnhqk', qr, kb).astype(jnp.float32) * scale + bias[None, None]
    lse = jax.nn.logsumexp(s, axis=-1)
    p = jnp.exp(s - lse[..., None])
    o = jnp.einsum('brnhqk,brnkhd->brnqhd', p, vb.astype(jnp.float32))

    o = o.reshape(B, dilation, L, H, Dh).transpose(0, 2, 1, 3, 4).reshape(B, s_pad, H, Dh)[:, :S]
    lse = lse.transpose(0, 1, 2, 4, 3).reshape(B, dilation, L, H).transpose(0, 2, 1, 3).reshape(B, s_pad, H)[:, :S]
    return o, lse

def _dilated_attention(q, k, v):
    slopes = _alibi_slopes(q.shape[2])
    outs, lses = [], []
    for window, dilation in DIL_CONFIGS:
        o, lse = _dilated_branch(q, k, v, slopes, window, dilation)
        outs.append(o)
        lses.append(lse)
    w = jax.nn.softmax(jnp.stack(lses, axis=0), axis=0)
    o = jnp.sum(w[..., None] * jnp.stack(outs, axis=0), axis=0)
    return o.astype(q.dtype)

def _forgetting_attention(q, k, v, log_f):
    B, S, H, Dh = q.shape
    nb = S // BLOCK
    c = jnp.cumsum(log_f, axis=1).transpose(0, 2, 1)
    qb = q.reshape(B, nb, BLOCK, H, Dh).transpose(1, 0, 2, 3, 4)
    cq = c.reshape(B, H, nb, BLOCK).transpose(2, 0, 1, 3)
    kpos = jnp.arange(S)
    scale = 1.0 / math.sqrt(Dh)

    def one_block(args):
        qblk, cblk, n = args
        s = jnp.einsum('bqhd,bkhd->bhqk', qblk, k).astype(jnp.float32) * scale
        s = s + (cblk[..., :, None] - c[:, :, None, :])
        qpos = n * BLOCK + jnp.arange(BLOCK)
        s = jnp.where((kpos[None, :] <= qpos[:, None])[None, None], s, NEG)
        p = jax.nn.softmax(s, axis=-1)
        return jnp.einsum('bhqk,bkhd->bqhd', p.astype(v.dtype), v)

    o = lax.map(one_block, (qb, cq, jnp.arange(nb)))
    return o.transpose(1, 0, 2, 3, 4).reshape(B, S, H, Dh)

def _hybrid_mixer(h, w_in, b_forget, w_out):
    B, S, _ = h.shape
    z = h @ w_in
    o0 = 3 * DIL_WIDTH
    o1 = o0 + 3 * FOX_WIDTH
    qa, ka, va = jnp.split(z[..., :o0], 3, axis=-1)
    qf, kf, vf = jnp.split(z[..., o0:o1], 3, axis=-1)
    gate = z[..., o1:]
    shp_a = (B, S, N_DIL_HEADS, HEAD_DIM)
    shp_f = (B, S, N_FOX_HEADS, HEAD_DIM)
    ya = _dilated_attention(qa.reshape(shp_a), ka.reshape(shp_a), va.reshape(shp_a))
    log_f = jax.nn.log_sigmoid(gate.astype(jnp.float32) + b_forget.astype(jnp.float32))
    yf = _forgetting_attention(qf.reshape(shp_f), kf.reshape(shp_f), vf.reshape(shp_f), log_f)
    y = jnp.concatenate([ya.reshape(B, S, DIL_WIDTH), yf.reshape(B, S, FOX_WIDTH).astype(ya.dtype)], axis=-1)
    return y @ w_out

def _cross_attention(h, m, w_xq, w_xk, w_xv, w_xo):
    B, S, _ = h.shape
    M = m.shape[1]
    q = (h @ w_xq).reshape(B, S, N_XATTN_HEADS, XATTN_HEAD_DIM)
    k = (m @ w_xk).reshape(B, M, N_XATTN_HEADS, XATTN_HEAD_DIM)
    v = (m @ w_xv).reshape(B, M, N_XATTN_HEADS, XATTN_HEAD_DIM)
    s = jnp.einsum('bqhd,bkhd->bhqk', q, k).astype(jnp.float32) / math.sqrt(XATTN_HEAD_DIM)
    p = jax.nn.softmax(s, axis=-1)
    o = jnp.einsum('bhqk,bkhd->bqhd', p.astype(v.dtype), v).reshape(B, S, N_XATTN_HEADS * XATTN_HEAD_DIM)
    return o @ w_xo

def _sq_relu_mlp(h, w_up, w_down):
    a = jax.nn.relu(h @ w_up)
    return (a * a) @ w_down

def setup_inputs(seed: int = 0) -> dict:
    key = jax.random.key(seed)
    ks = jax.random.split(key, 16)
    f32 = jnp.float32

    def w(k, shape):
        return jax.random.normal(k, shape, f32) * shape[0] ** -0.5

    def gain(k):
        return 1.0 + 0.05 * jax.random.normal(k, (D_MODEL,), f32)

    return {
        "x": jax.random.normal(ks[0], (BATCH, SEQ, D_MODEL), f32),
        "mem": jax.random.normal(ks[1], (BATCH, N_MEM, D_MODEL), f32),
        "g_mix": gain(ks[2]),
        "w_in": w(ks[3], (D_MODEL, IN_WIDTH)),
        "b_forget": 0.1 * jax.random.normal(ks[4], (N_FOX_HEADS,), f32),
        "w_out": w(ks[5], (MIX_WIDTH, D_MODEL)),
        "g_xattn": gain(ks[6]),
        "g_mem": gain(ks[7]),
        "w_xq": w(ks[8], (D_MODEL, N_XATTN_HEADS * XATTN_HEAD_DIM)),
        "w_xk": w(ks[9], (D_MODEL, N_XATTN_HEADS * XATTN_HEAD_DIM)),
        "w_xv": w(ks[10], (D_MODEL, N_XATTN_HEADS * XATTN_HEAD_DIM)),
        "w_xo": w(ks[11], (N_XATTN_HEADS * XATTN_HEAD_DIM, D_MODEL)),
        "g_mlp": gain(ks[12]),
        "w_up": w(ks[13], (D_MODEL, D_FF)),
        "w_down": w(ks[14], (D_FF, D_MODEL)),
        "g_final": gain(ks[15]),
    }

def reference(x, mem, g_mix, w_in, b_forget, w_out, g_xattn, g_mem, w_xq, w_xk, w_xv, w_xo,
              g_mlp, w_up, w_down, g_final):
    m = _rmsnorm(mem, g_mem)
    for _ in range(DEPTH):
        x = x + _hybrid_mixer(_rmsnorm(x, g_mix), w_in, b_forget, w_out)
        x = x + _cross_attention(_rmsnorm(x, g_xattn), m, w_xq, w_xk, w_xv, w_xo)
        x = x + _sq_relu_mlp(_rmsnorm(x, g_mlp), w_up, w_down)
    return _rmsnorm(x, g_final)


_drawn_inputs = setup_inputs


def setup_inputs(seed=0):
    import zlib

    import numpy as np

    out = dict(_drawn_inputs(seed))
    spreads = {}
    factors = {'b_forget': 2.707, 'g_xattn': 8.0, 'g_mem': 7.854, 'g_mlp': 6.335}
    for name, (base, spread) in spreads.items():
        noise = np.random.default_rng([zlib.crc32(name.encode()), seed]).standard_normal(out[name].shape)
        drawn = base * np.exp(spread * noise) if base else spread * noise
        out[name] = __import__('jax').numpy.asarray(drawn.astype(out[name].dtype))
    for name, factor in factors.items():
        out[name] = (out[name] * factor).astype(out[name].dtype)
    return out
```

```python
import math
from contextlib import ExitStack

import numpy as np

import concourse.bass as bass
from concourse import mybir

P = 128
T = 1024
D = 1024
KT = D // P
TT = T // P
HALF = 512
N_MEM = 256
MT = N_MEM // P
HEAD = 64
PAIRS = 8
STEPS = 16
QB = T // P
X_HEADS = 4
D_FF = 4096
GROUPS = D_FF // HALF
EPS = 1e-6
NEG = -1e30
DILATIONS = ((128, 1), (512, 4), (2048, 16))
GATE_COL = 6 * PAIRS // 2 * P
KB = 1024


def dilated_steps(has_next):
    order = []
    done = 0
    total = 144 if has_next else 0
    for u in range(STEPS):
        order.append(("T", u))
        if u + 1 < STEPS or has_next:
            order.append(("QK", u + 1))
        if u == 0:
            order += [("V", 0), ("V", 1)]
        for part, share in ((0, 0.6), (1, 1.0)):
            upto = round(total * (u + share) / STEPS) if u < STEPS - 1 or part == 0 else total
            while done < upto:
                stop = min(upto, (done // 24 + 1) * 24)
                order.append(("G", done, stop))
                if stop % 24 == 0:
                    order.append(("tile", stop // 24 - 1))
                done = stop
            if part == 0:
                order.append(("PV", u))
    return order


def hybrid_layer(nc, x, mem, g_mix, w_in, b_forget, w_out, g_xattn, g_mem, w_xq, w_xk, w_xv, w_xo,
                 g_mlp, w_up, w_down, g_final, ident_c, masks_c, alibi_c, out):
    f32, f32r = mybir.dt.float32, mybir.dt.float32r
    ALU, ACT, AX = mybir.AluOpType, mybir.ActivationFunctionType, mybir.AxisListType

    x_t = x[0].rearrange("(t p) d -> t p d", p=P)
    out_t = out[0].rearrange("(t p) d -> t p d", p=P)
    mem_t = mem[0].rearrange("(t p) d -> t p d", p=P)

    def k_rows(w):
        return w.rearrange("(k p) n -> p k n", p=P)

    w_in_k, w_out_k, w_xq_k, w_xk_k, w_xv_k, w_xo_k, w_up_k = map(
        k_rows, (w_in, w_out, w_xq, w_xk, w_xv, w_xo, w_up))
    bias_rows = nc.dram_tensor("bias_rows", (2 * PAIRS, T), f32).ap()

    base = 16 * KB + 512

    def at(name, shape, dt, kb):
        return nc.alloc_sbuf_tensor_at(name, shape, dt, offset=base + int(kb * KB))

    act_hi = at("act_hi", [P, KT, T], f32r, 0)
    act_lo = at("act_lo", [P, KT, T], f32r, 32)
    X = at("X", [P, TT, D], f32, 64)
    ident = at("ident", [P, P], f32, 96)
    row_max = at("row_max", [P, 2], f32, 96.5)
    row_sum = at("row_sum", [P, 2], f32, 96.5625)
    sum_sq = at("sum_sq", [P, 2], f32, 96.625)
    var = at("var", [P, 2], f32, 96.6875)
    std = at("std", [P, 2], f32, 96.75)
    rstd0 = at("rstd0", [P, 2], f32, 96.8125)
    newt = at("newt", [P, 2, 2], f32, 96.875)
    rstd = at("rstd", [P, 2], f32, 96.9375)
    x_max = at("x_max", [P, 2, X_HEADS], f32, 97)
    x_neg = at("x_neg", [P, 2, X_HEADS], f32, 97.0625)
    x_sum = at("x_sum", [P, 2, X_HEADS], f32, 97.125)
    x_inv = at("x_inv", [P, 2, X_HEADS], f32, 97.1875)
    b_col = at("b_col", [8, 1], f32, 97.25)
    row_inv = at("row_inv", [P, 2], f32, 97.3125)
    slot_kb = [98, 106, 114, 134, 142, 150, 158, 166]
    w_hi = [at(f"w_hi{i}", [P, 1024], f32r, kb) for i, kb in enumerate(slot_kb)]
    w_lo = [at(f"w_lo{i}", [P, 1024], f32r, kb + 4) for i, kb in enumerate(slot_kb)]
    raw = [at(f"raw{i}", [P, 1024], f32, 122 + 4 * i) for i in range(3)]
    qA = [[at(f"qA{a}{h}", [HEAD + 1, T], f32, 134 + 16 * a + 4 * h) for h in range(2)] for a in range(2)]
    kA = [[at(f"kA{a}{h}", [HEAD + 1, T], f32, 142 + 16 * a + 4 * h) for h in range(2)] for a in range(2)]
    V = [at(f"V{a}", [P, TT, P], f32, 166 + 4 * a) for a in range(2)]
    vT = at("vT", [P, T], f32, 174)
    S = [at(f"S{a}", [P, T], f32, 178 + 4 * a) for a in range(2)]
    pT = at("pT", [P, T], f32, 186)
    mask = at("mask", [P, T], f32, 190)
    gate_raw = at("gate_raw", [P, 1024], f32, 194)
    gate_hi = at("gate_hi", [P, 1024], f32r, 198)
    gate_lo = at("gate_lo", [P, 1024], f32r, 202)
    gate_z = at("gate_z", [8, T], f32, 178)
    gate_e = at("gate_e", [8, T], f32, 182)
    gate_l = at("gate_l", [8, T], f32, 186)
    a_hn = [at(f"a_hn{i}", [P, D], f32, 166 + 4 * i) for i in range(2)]
    a_gain = at("a_gain", [P, D], f32, 174)
    c_hn = [at(f"c_hn{i}", [P, D], f32, 174 + 4 * i) for i in range(2)]
    c_gain = at("c_gain", [P, D], f32, 182)
    m_gain = at("m_gain", [P, D], f32, 186)
    m_in = at("m_in", [P, MT, D], f32, 134)
    mT_hi = at("mT_hi", [P, KT, N_MEM], f32r, 190)
    mT_lo = at("mT_lo", [P, KT, N_MEM], f32r, 198)
    kx = at("kx", [P, KT, N_MEM], f32, 174)
    vx = at("vx", [P, MT, D], f32, 182)
    vxT = at("vxT", [P, 2, N_MEM], f32, 130)
    qx = at("qx", [P, KT, T], f32, 142)
    Sx = [at(f"Sx{i}", [P, X_HEADS, N_MEM], f32, 134 + 4 * i) for i in range(2)]
    pTx = at("pTx", [P, 2 * X_HEADS, HALF], f32, 190)
    r_ff = at("r_ff", [P, 2, HALF], f32, 130)
    a_hi = at("a_hi", [P, 4, T], f32r, 174)
    a_lo = at("a_lo", [P, 4, T], f32r, 190)
    f_hn = [at(f"f_hn{i}", [P, D], f32, 98 + 4 * i) for i in range(2)]
    f_gain = at("f_gain", [P, D], f32, 106)

    with ExitStack() as ctx:
        def sem(name):
            return ctx.enter_context(nc.semaphore(name))

        psS = [ctx.enter_context(nc.psum_tensor(f"psS{i}", [P, 1024], f32)) for i in range(2)]
        psG = [ctx.enter_context(nc.psum_tensor(f"psG{i}", [P, HALF], f32)) for i in range(2)]
        psO = [ctx.enter_context(nc.psum_tensor(f"psO{i}", [P, HALF], f32)) for i in range(2)]

        consts_loaded = sem("consts_loaded")
        b_loaded = sem("b_loaded")
        alibi_stored = sem("alibi_stored")
        gain_loaded = [sem(f"gain_loaded{i}") for i in range(5)]
        x_loaded = [sem(f"x_loaded{i}") for i in range(TT)]
        m_loaded = [sem(f"m_loaded{i}") for i in range(MT)]
        ones_set = sem("ones_set")
        rawB = [sem(f"rawB_loaded{i}") for i in range(3)]
        rawC = [sem(f"rawC_loaded{i}") for i in range(2)]
        gate_zeroed = sem("gate_zeroed")
        gate_loaded = sem("gate_loaded")
        gate_hi_done = sem("gate_hi_done")
        gate_lo_done = sem("gate_lo_done")
        gate_act = sem("gate_act")
        gate_dve = sem("gate_dve")
        cum_stored = sem("cum_stored")
        bias_loaded = [sem(f"bias_loaded{i}") for i in range(2)]
        mask_loaded = sem("mask_loaded")
        hi_done = sem("hi_done")
        lo_done = sem("lo_done")
        tile_done = sem("tile_done")
        tile_out = sem("tile_out")
        qk_done = sem("qk_done")
        max_gate = sem("max_gate")
        max_done = sem("max_done")
        exp_done = sem("exp_done")
        inv_done = sem("inv_done")
        tr_done = sem("tr_done")
        pT_done = sem("pT_done")
        pv_done = sem("pv_done")
        o_out = sem("o_out")
        yt_done = sem("yt_done")
        y_hi = sem("y_hi")
        y_lo = sem("y_lo")
        n_sq = sem("n_sq")
        n_var = sem("n_var")
        n_std = sem("n_std")
        n_chain = sem("n_chain")
        n_hn = sem("n_hn")
        n_tr = sem("n_tr")
        n_hi = sem("n_hi")
        n_lo = sem("n_lo")
        sx_done = sem("sx_done")
        sx_max = sem("sx_max")
        sx_neg = sem("sx_neg")
        sx_exp = sem("sx_exp")
        sx_inv = sem("sx_inv")
        sx_norm = sem("sx_norm")
        sx_tr = sem("sx_tr")
        sx_pT = sem("sx_pT")
        hi_out = sem("hi_out")
        relu_out = sem("relu_out")
        sq_out = sem("sq_out")
        out_stored = [sem(f"out_stored{i}") for i in range(2)]

        PRO_TILES = 8
        B_TILES = PRO_TILES + 7 * 8 + 2
        B_BLOCKS = 3 * PAIRS

        def body_tile(p, j):
            return p * 8 + (PRO_TILES + j + 1)

        N_C, N_M, N_X, N_F = TT, 2 * TT, 2 * TT + MT, 3 * TT + MT
        C_OUT, C_XK, C_XV, C_XQ, C_XO, C_MLP = 0, 8, 16, 24, 32, 40
        G_OUT = B_TILES
        G_XK = G_OUT + 2 * TT
        G_XV = G_XK + KT
        G_XQ = G_XV + 2 * KT
        G_PV = G_XQ + 2 * KT
        G_XO = G_PV + 2 * KT
        G_MLP = G_XO + 2 * TT
        MLP_TILES = 8 + 2 * TT

        block = ctx.enter_context(nc.Block())

        def pair_cols(w, p, j):
            if isinstance(p, int):
                c = (p // 4) * 1536 + j * 512 + (p % 4) * P
                return w[:, :, c:c + P]
            return w[:, :, bass.ds((p // 4) * 1024 + p * P + j * 512, P)]

        @block.sync
        def _(sp):
            def gain(i, dst, g):
                sp.dma_start(dst[:], g.rearrange("(a d) -> a d", a=1).to_broadcast([P, D])).then_inc(gain_loaded[i], 16)

            def raw_pair(p, j):
                src = pair_cols(w_in_k, p, j)
                sp.dma_start(raw[j][:].rearrange("p (k n) -> p k n", n=P), src).then_inc(rawB[j], 16)

            def bias(p, par):
                for h in range(2):
                    sp.dma_start(kA[par][h][HEAD:HEAD + 1, :], bias_rows[bass.ds(p * 2 + h, 1), :]).then_inc(bias_loaded[par], 16)

            def raw_block(m, i, src, shape):
                sp.wait_ge(lo_done, m + (B_BLOCKS - 1))
                sp.dma_start(shape(raw[i]), src).then_inc(rawC[i], 16)

            for t in range(TT):
                if t == 1:
                    gain(0, a_gain, g_mix)
                    sp.dma_start(ident[:], ident_c).then_inc(consts_loaded, 16)
                sp.dma_start(X[:, t, :], x_t[t]).then_inc(x_loaded[t], 16)
                if t == 3:
                    for j in range(3):
                        raw_pair(0, j)
            sp.dma_start(b_col[:], b_forget.rearrange("(h a) -> h a", a=1)).then_inc(b_loaded, 16)
            sp.dma_start(bias_rows[0:PAIRS, :], alibi_c).then_inc(alibi_stored, 16)
            sp.dma_start(mask[:], masks_c[0]).then_inc(mask_loaded, 16)
            sp.wait_ge(gate_zeroed, 1)
            sp.dma_start(gate_raw[:].rearrange("p (k n) -> p k n", n=P)[:, :, 0:8],
                         w_in_k[:, :, GATE_COL:GATE_COL + 8]).then_inc(gate_loaded, 16)
            sp.wait_ge(alibi_stored, 16)
            bias(0, 0)
            for j in range(3):
                sp.wait_ge(lo_done, j + 1)
                raw_pair(1, j)
            sp.wait_ge(gate_dve, 3)
            sp.dma_start(bias_rows[PAIRS:2 * PAIRS, :], gate_l[:]).then_inc(cum_stored, 16)
            sp.wait_ge(cum_stored, 16)

            def pair_loads(it, p, par):
                sp.wait_ge(qk_done, p * 16 + 1)
                if True:
                    bias(p + 1, 1 - par)
                if not isinstance(p, int):
                    for j in range(3):
                        sp.wait_ge(lo_done, p * 3 + (3 + j + 1))
                        raw_pair(p + 2, j)
                    if par == 1:
                        sp.wait_ge(max_done, p * 16 + 16)
                        sp.dma_start(mask[:], masks_c[bass.ds(it + 1, 1), :, :].rearrange("o p n -> (o p) n")).then_inc(mask_loaded, 16)

            with sp.Fori(0, 3) as it:
                for par in range(2):
                    pair_loads(it, it * 2 + par, par)
            pair_loads(3, 6, 0)
            def two_rows(w, half, i):
                return w[:, 2 * i:2 * i + 2, half * HALF:(half + 1) * HALF]

            def rows(r):
                return r[:].rearrange("p (k n) -> p k n", n=HALF)

            def cols(r):
                return r[:].rearrange("p (k n) -> p k n", n=P)

            sp.wait_ge(lo_done, B_BLOCKS)
            def out_block(m):
                raw_block(C_OUT + m, m % 2, two_rows(w_out_k, m // 4, m % 4), rows)

            for m in range(6):
                out_block(m)
            for t in range(TT):
                sp.wait_ge(yt_done, t + 1)
                sp.dma_start(X[:, t, :], x_t[t]).then_inc(x_loaded[t], 16)
                if t in (1, 2):
                    out_block(5 + t)
            gain(1, c_gain, g_xattn)
            gain(2, m_gain, g_mem)
            sp.wait_ge(tile_done, G_OUT + TT)
            for t in range(MT):
                sp.dma_start(m_in[:, t, :], mem_t[t]).then_inc(m_loaded[t], 16)
            for first, w in ((C_XK, w_xk_k), (C_XV, w_xv_k), (C_XQ, w_xq_k)):
                with sp.Fori(0, 4) as c:
                    for i in range(2):
                        raw_block(c * 2 + (first + i), i, w[:, :, bass.ds(c * 256 + i * P, P)], cols)
            for m in range(8):
                raw_block(C_XO + m, m % 2, two_rows(w_xo_k, m // 4, m % 4), rows)
                if m == 3:
                    sp.wait_ge(tile_done, G_PV + 2 * KT)
                    gain(3, c_gain, g_mlp)
            with sp.Fori(0, GROUPS) as g:
                for i in range(8):
                    if i < 4:
                        raw_block(g * 8 + (C_MLP + i), i % 2, w_up_k[:, :, bass.ds(g * HALF + i * P, P)], cols)
                    else:
                        raw_block(g * 8 + (C_MLP + i), i % 2, w_down[bass.ds(g * HALF + (i - 4) * P, P), :], lambda r: r[:])
            sp.wait_ge(tile_done, G_MLP + GROUPS * MLP_TILES)
            gain(4, f_gain, g_final)
            for t in range(TT):
                sp.wait_ge(n_hn, N_F + t + 1)
                sp.dma_start(out_t[t], f_hn[t % 2][:]).then_inc(out_stored[t % 2], 16)
            for i in range(2):
                sp.wait_ge(out_stored[i], 16 * TT // 2)

        @block.tensor
        def _(pe):
            def split_products(dst, parts, last_inc=None):
                n = len(parts)
                for k, (sh, sl, mh, ml) in enumerate(parts):
                    nc.tensor.matmul(dst, sh, mh, start=(k == 0), stop=False)
                    nc.tensor.matmul(dst, sh, ml, start=False, stop=False)
                    mm = nc.tensor.matmul(dst, sl, mh, start=False, stop=(k == n - 1))
                return mm

            def col_block(slot_hi, slot_lo, k):
                return slot_hi[:, k * P:(k + 1) * P], slot_lo[:, k * P:(k + 1) * P]

            def proj(p_tile, i0, i1, slots):
                for i in range(i0, i1):
                    j, r = divmod(i, 24)
                    k, part = divmod(r, 3)
                    chunk, half = divmod(j, 2)
                    sh, sl = slots[chunk]
                    hi, lo = col_block(sh, sl, k)
                    mh = act_hi[:, k, half * HALF:(half + 1) * HALF]
                    ml = act_lo[:, k, half * HALF:(half + 1) * HALF]
                    a, b = ((hi, mh), (hi, ml), (lo, mh))[part]
                    mm = nc.tensor.matmul(psG[j % 2][:], a, b, start=(r == 0), stop=(r == 23))
                    if r == 23:
                        mm.then_inc(tile_done, 1)

            def scores(par, h, qb, s):
                n = (qb + 1) * P
                for c in range(0, n, HALF):
                    w = min(HALF, n - c)
                    mm = nc.tensor.matmul(psS[s % 2][:, c:c + w], qA[par][h][:, qb * P:(qb + 1) * P],
                                          kA[par][h][:, c:c + w], start=True, stop=True)
                mm.then_inc(qk_done, 1)

            def norm_tr(n, src):
                pe.wait_ge(n_hn, n + 1)
                if n >= 2:
                    pe.wait_ge(n_lo, n - 1)
                for k in range(KT):
                    mm = nc.tensor.transpose(psS[n % 2][:, k * P:(k + 1) * P], src[:, k * P:(k + 1) * P], ident[:])
                mm.then_inc(n_tr, 1)

            pe.wait_ge(consts_loaded, 16)
            for t in range(TT):
                norm_tr(t, a_hn[t % 2])
            slots = [(w_hi[j], w_lo[j]) for j in range(3)] + [(gate_hi, gate_lo)]
            for j in range(8):
                if j == 0:
                    pe.wait_ge(n_lo, 4)
                if j == 1:
                    pe.wait_ge(n_lo, TT)
                if j % 2 == 0 and j < 6:
                    pe.wait_ge(lo_done, j // 2 + 1)
                if j == 6:
                    pe.wait_ge(gate_lo_done, 1)
                if j >= 2:
                    pe.wait_ge(tile_out, j - 1)
                proj(0, j * 24, j * 24 + 24, slots)
            pe.wait_ge(bias_loaded[0], 32)
            pe.wait_ge(ones_set, 4)
            pe.wait_ge(tile_out, 8)
            scores(0, 0, 0, 0)

            def pair_pe(p, par, has_next):
                for ev in dilated_steps(has_next):
                    kind, u = ev[0], ev[1]
                    h, qb = divmod(u % STEPS, QB)
                    if kind == "T":
                        pe.wait_ge(exp_done, p * 16 + (u + 1))
                        for b in range(qb + 1):
                            mm = nc.tensor.transpose(psS[u % 2][:, b * P:(b + 1) * P], S[u % 2][:, b * P:(b + 1) * P], ident[:])
                        mm.then_inc(tr_done, 1)
                    elif kind == "QK":
                        if u >= 2:
                            pe.wait_ge(pT_done, p * 16 + (u - 1))
                        if u == STEPS:
                            pe.wait_ge(tile_out, body_tile(p, 5))
                            pe.wait_ge(bias_loaded[1 - par], bias_count(p, par))
                            scores(1 - par, 0, 0, u)
                        else:
                            scores(par, h, qb, u)
                    elif kind == "V":
                        if u == 0:
                            pe.wait_ge(tile_out, body_tile(p, -1))
                        for b in range(4):
                            c = (4 * u + b) * P
                            mm = nc.tensor.transpose(psG[u][:, b * P:(b + 1) * P], vT[:, c:c + P], ident[:])
                        mm.then_inc(tile_done, 1)
                    elif kind == "G":
                        i0, i1 = ev[1], ev[2]
                        j = i0 // 24
                        if i0 % 24 == 0:
                            pe.wait_ge(tile_out, body_tile(p, j))
                            if j % 2 == 0:
                                pe.wait_ge(lo_done, p * 3 + (3 + j // 2 + 1))
                        proj(None, i0, i1, slots)
                    elif kind == "PV":
                        if u == 0:
                            pe.wait_ge(tile_out, body_tile(p, 1))
                        pe.wait_ge(pT_done, p * 16 + (u + 1))
                        if u >= 2:
                            pe.wait_ge(o_out, p * 16 + (u - 1))
                        for b in range(qb + 1):
                            mm = nc.tensor.matmul(psO[u % 2][:, 0:HEAD], pT[:, b * P:(b + 1) * P],
                                                  V[par][:, b, h * HEAD:(h + 1) * HEAD], start=(b == 0), stop=(b == qb))
                        mm.then_inc(pv_done, 1)

            def bias_count(p, par):
                if isinstance(p, int):
                    return 32 * ((p + 1) // 2 + 1)
                return (p + (2 + par)) * 16

            with pe.Fori(0, 3) as it:
                for par in range(2):
                    pair_pe(it * 2 + par, par, True)
            pair_pe(6, 0, True)
            pair_pe(7, 1, False)

            def token_tile(psum, t, half, base_slot):
                parts = []
                for k in range(KT):
                    sh, sl = w_hi[base_slot + k // 2], w_lo[base_slot + k // 2]
                    o = (k % 2) * HALF
                    tok = slice(t * P, (t + 1) * P)
                    parts.append((act_hi[:, k, tok], act_lo[:, k, tok], sh[:, o:o + HALF], sl[:, o:o + HALF]))
                return split_products(psum[:], parts)

            def residual_product(g0, block0, n0, before):
                for half in range(2):
                    for t in range(TT):
                        g = g0 + half * TT + t
                        before(half, t)
                        if t == 0:
                            pe.wait_ge(lo_done, B_BLOCKS + block0 + 4 * half + 4)
                        pe.wait_ge(tile_out, g - 1)
                        token_tile(psG[g % 2], t, half, 4 * half).then_inc(tile_done, 1)
                        if half and t >= 2:
                            norm_tr(n0 + t - 2, c_hn[(n0 + t) % 2])
                norm_tr(n0 + TT - 2, c_hn[n0 % 2])
                norm_tr(n0 + TT - 1, c_hn[(n0 + 1) % 2])

            def y_transposes(t):
                pe.wait_ge(o_out, PAIRS * STEPS)
                pe.wait_ge(pT_done, PAIRS * STEPS)
                if t >= 2:
                    pe.wait_ge(y_lo, t - 1)
                for k in range(KT):
                    mm = nc.tensor.transpose(psS[t % 2][:, k * P:(k + 1) * P], X[:, t, k * P:(k + 1) * P], ident[:])
                mm.then_inc(yt_done, 1)

            def before_out(half, t):
                if half == 0:
                    if t == 0:
                        y_transposes(0)
                    if t + 1 < TT:
                        y_transposes(t + 1)
                    pe.wait_ge(y_lo, t + 1)
            residual_product(G_OUT, C_OUT, N_C, before_out)
            for t in range(MT):
                norm_tr(N_M + t, c_hn[t % 2])

            def mem_chunk(g, slot):
                return split_products(psG[g % 2][:, 0:N_MEM],
                                      [(*col_block(w_hi[slot], w_lo[slot], k), mT_hi[:, k, :], mT_lo[:, k, :]) for k in range(KT)])

            pe.wait_ge(n_lo, N_M + MT)
            with pe.Fori(0, 4) as c:
                for i in range(2):
                    pe.wait_ge(lo_done, c * 2 + (B_BLOCKS + C_XK + i + 1))
                    pe.wait_ge(tile_out, c * 2 + (G_XK + i - 1))
                    mem_chunk(G_XK + i, i).then_inc(tile_done, 1)

            with pe.Fori(0, 4) as c:
                for i in range(2):
                    pe.wait_ge(lo_done, c * 2 + (B_BLOCKS + C_XV + i + 1))
                    pe.wait_ge(tile_out, c * 4 + (G_XV + 2 * i - 1))
                    mem_chunk(G_XV, i).then_inc(tile_done, 1)
                    pe.wait_ge(tile_out, c * 4 + (G_XV + 2 * i + 1))
                    for b in range(MT):
                        mm = nc.tensor.transpose(psG[1][:, b * P:(b + 1) * P], vxT[:, i, b * P:(b + 1) * P], ident[:])
                    mm.then_inc(tile_done, 1)

            with pe.Fori(0, 4) as c:
                for i in range(2):
                    pe.wait_ge(lo_done, c * 2 + (B_BLOCKS + C_XQ + i + 1))
                    for half in range(2):
                        pe.wait_ge(tile_out, c * 4 + (G_XQ + 2 * i + half - 1))
                        tok = slice(half * HALF, (half + 1) * HALF)
                        split_products(psG[half][:], [(*col_block(w_hi[i], w_lo[i], k), act_hi[:, k, tok], act_lo[:, k, tok])
                                                      for k in range(KT)]).then_inc(tile_done, 1)

            def x_scores(t):
                if t >= 2:
                    pe.wait_ge(sx_pT, t - 1)
                for h in range(X_HEADS):
                    for c in range(2):
                        mm = nc.tensor.matmul(psS[t % 2][:, h * N_MEM:(h + 1) * N_MEM], qx[:, 2 * h + c, t * P:(t + 1) * P],
                                              kx[:, 2 * h + c, :], start=(c == 0), stop=(c == 1))
                mm.then_inc(sx_done, 1)

            def x_transposes(t):
                pe.wait_ge(sx_norm, t + 1)
                for b in range(2 * X_HEADS):
                    h, c = divmod(b, 2)
                    mm = nc.tensor.transpose(psS[t % 2][:, b * P:(b + 1) * P], Sx[t % 2][:, h, c * P:(c + 1) * P], ident[:])
                mm.then_inc(sx_tr, 1)

            def x_outputs(half):
                pe.wait_ge(sx_pT, 4 * half + 4)
                for j in range(KT):
                    g = G_PV + half * KT + j
                    pe.wait_ge(tile_out, g - 1)
                    h = j // 2
                    for c in range(MT):
                        mm = nc.tensor.matmul(psG[g % 2][:], vx[:, c, j * P:(j + 1) * P], pTx[:, 2 * h + c, :],
                                              start=(c == 0), stop=(c == MT - 1))
                    mm.then_inc(tile_done, 1)

            pe.wait_ge(tile_out, G_PV)
            pe.wait_ge(n_lo, N_M + MT)
            x_scores(0)
            x_scores(1)
            for t in range(TT):
                x_transposes(t)
                if t + 2 < TT:
                    x_scores(t + 2)
                if t % 4 == 3:
                    x_outputs(t // 4)

            def before_xo(half, t):
                if half == 0 and t == 0:
                    pe.wait_ge(tile_out, G_PV + 2 * KT)
            residual_product(G_XO, C_XO, N_X, before_xo)

            pe.wait_ge(n_lo, N_X + TT)
            with pe.Fori(0, GROUPS) as g:
                for c in range(4):
                    pe.wait_ge(lo_done, g * 8 + (B_BLOCKS + C_MLP + c + 1))
                    for half in range(2):
                        pe.wait_ge(tile_out, g * MLP_TILES + (G_MLP + 2 * c + half - 1))
                        tok = slice(half * HALF, (half + 1) * HALF)
                        split_products(psG[half][:], [(*col_block(w_hi[c], w_lo[c], k), act_hi[:, k, tok], act_lo[:, k, tok])
                                                      for k in range(KT)]).then_inc(tile_done, 1)
                for t in range(TT):
                    for half in range(2):
                        j = 8 + 2 * t + half
                        cs = slice(half * HALF, (half + 1) * HALF)
                        if t == 0 and half == 0:
                            pe.wait_ge(lo_done, g * 8 + (B_BLOCKS + C_MLP + 8))
                        pe.wait_ge(tile_out, g * MLP_TILES + (G_MLP + j - 1))
                        tok = slice(t * P, (t + 1) * P)
                        split_products(psG[half][:], [(a_hi[:, c, tok], a_lo[:, c, tok], w_hi[4 + c][:, cs], w_lo[4 + c][:, cs])
                                                      for c in range(4)]).then_inc(tile_done, 1)

        @block.scalar
        def _(act):
            def split_hi(dst, src, sem_, *waits):
                for s_, v in waits:
                    act.wait_ge(s_, v)
                nc.scalar.activation(dst, src, ACT.Copy).then_inc(sem_, 1)

            def sq(n, src, junk, *waits):
                for s_, v in waits:
                    act.wait_ge(s_, v)
                nc.scalar.activation(junk[:], src, ACT.Square, accum_out=sum_sq[:, n % 2:n % 2 + 1]).then_inc(n_sq, 1)

            def root(n):
                i = slice(n % 2, n % 2 + 1)
                act.wait_ge(n_var, n + 1)
                nc.scalar.activation(std[:, i], var[:, i], ACT.Sqrt).then_inc(n_std, 1)

            def norm_hi(n, dst):
                act.wait_ge(n_tr, n + 1)
                nc.scalar.activation(dst, psS[n % 2][:].rearrange("p (k t) -> p k t", t=P), ACT.Copy).then_inc(n_hi, 1)

            def act_tile(t):
                return act_hi[:, :, t * P:(t + 1) * P]

            for t in range(TT):
                if t >= 2:
                    sq(t, X[:, t, :], a_hn[t % 2], (n_tr, t - 1), (x_loaded[t], 16))
                else:
                    sq(t, X[:, t, :], a_hn[t % 2], (x_loaded[t], 16))
                root(t)
                if t >= 1:
                    norm_hi(t - 1, act_tile(t - 1))
                if t == 3:
                    for j in range(3):
                        split_hi(w_hi[j][:], raw[j][:], hi_done, (rawB[j], 16))
            norm_hi(TT - 1, act_tile(TT - 1))
            split_hi(gate_hi[:], gate_raw[:], gate_hi_done, (gate_loaded, 16))
            for j in range(3):
                split_hi(w_hi[j][:], raw[j][:], hi_done, (rawB[j], 32), (tile_done, 2 * j + 2))
            act.wait_ge(b_loaded, 16)
            for half in range(2):
                act.wait_ge(tile_done, 7 + half)
                nc.scalar.activation(gate_z[:, half * HALF:(half + 1) * HALF], psG[half][0:8, :], ACT.Identity,
                                     bias=b_col[:]).then_inc(gate_act, 1)
            act.wait_ge(gate_act, 2)
            nc.scalar.activation(gate_e[:], gate_z[:], ACT.Abs).then_inc(gate_act, 1)
            act.wait_ge(gate_act, 3)
            nc.scalar.activation(gate_e[:], gate_e[:], ACT.Exp, scale=-1.0).then_inc(gate_act, 1)
            act.wait_ge(gate_act, 4)
            nc.scalar.activation(gate_e[:], gate_e[:], ACT.Ln, bias=1.0).then_inc(gate_act, 1)

            def exp_step(u, value):
                n = (u % QB + 1) * P
                act.wait_ge(max_done, value)
                nc.scalar.activation(S[u % 2][:, 0:n], S[u % 2][:, 0:n], ACT.Exp, bias=row_max[:, u % 2:u % 2 + 1], scale=-1.0,
                                     accum_out=row_sum[:, u % 2:u % 2 + 1]).then_inc(exp_done, 1)

            exp_step(0, 1)

            def pair_act(p, par, has_next, splits):
                for ev in dilated_steps(has_next):
                    kind, u = ev[0], ev[1]
                    if kind == "T":
                        n = (u % QB + 1) * P
                        act.wait_ge(tr_done, p * 16 + (u + 1))
                        nc.scalar.activation(pT[:, 0:n], psS[u % 2][:, 0:n], ACT.Copy).then_inc(pT_done, 1)
                    elif kind == "QK":
                        exp_step(u, p * 16 + (u + 1))
                    elif kind == "tile" and u % 2 == 1 and splits:
                        j = u // 2
                        act.wait_ge(tile_done, body_tile(p, u + 2))
                        split_hi(w_hi[j][:], raw[j][:], hi_done, (rawB[j], p * 16 + 48))

            with act.Fori(0, 3) as it:
                for par in range(2):
                    pair_act(it * 2 + par, par, True, True)
            pair_act(6, 0, True, False)
            act.wait_ge(tile_done, body_tile(6, 7))

            def block_hi(m, i, slot, value=None):
                act.wait_ge(rawC[i], value if value is not None else 16 * (m // 2 + 1))
                nc.scalar.activation(w_hi[slot][:], raw[i][:], ACT.Copy).then_inc(hi_done, 1)

            for m in range(3):
                block_hi(C_OUT + m, m % 2, m)
            pair_act(7, 1, False, False)
            act.wait_ge(pv_done, PAIRS * STEPS)
            block_hi(C_OUT + 3, 1, 3)

            for t in range(TT):
                act.wait_ge(yt_done, t + 1)
                nc.scalar.activation(act_tile(t), psS[t % 2][:].rearrange("p (k t) -> p k t", t=P), ACT.Copy).then_inc(y_hi, 1)
                if t in (1, 2, 3, 4):
                    block_hi(C_OUT + 3 + t, (3 + t) % 2, 3 + t)

            def residual_norm_act(g0, n0, extra):
                for t in range(TT):
                    n = n0 + t
                    sq(n, X[:, t, :], c_hn[n % 2], (n_tr, n - 1), (tile_out, g0 + TT + t + 1))
                    root(n)
                    if t >= 2:
                        norm_hi(n - 2, act_tile(t - 2))
                    extra(t)

            def extra_c(t):
                if t in (2, 3):
                    block_hi(C_XK + t - 2, t - 2, t - 2)

            residual_norm_act(G_OUT, N_C, extra_c)
            for t in range(MT):
                n = N_M + t
                sq(n, m_in[:, t, :], c_hn[n % 2], (n_tr, n - 1), (m_loaded[t], 16))
                root(n)
                norm_hi(n - 2, act_tile(TT - 2 + t))
            for t in range(MT):
                norm_hi(N_M + t, mT_hi[:, :, t * P:(t + 1) * P])

            with act.Fori(0, 4) as c:
                for i in range(2):
                    act.wait_ge(tile_done, c * 2 + (G_XK + i + 1))
                    block_hi(None, i, i, c * 16 + 16 * ((C_XK + 2) // 2 + 1))
            with act.Fori(0, 4) as c:
                for i in range(2):
                    act.wait_ge(tile_done, c * 4 + (G_XV + 2 * i + 1))
                    block_hi(None, i, i, c * 16 + 16 * ((C_XV + 2) // 2 + 1))
            with act.Fori(0, 4) as c:
                for i in range(2):
                    act.wait_ge(tile_done, c * 4 + (G_XQ + 2 * i + 2))
                    block_hi(None, i, i, c * 16 + 16 * ((C_XQ + 2) // 2 + 1))
            block_hi(C_XO + 2, 0, 2)

            def x_exp(t):
                act.wait_ge(sx_neg, t + 1)
                for h in range(X_HEADS):
                    e = nc.scalar.activation(Sx[t % 2][:, h, :], psS[t % 2][:, h * N_MEM:(h + 1) * N_MEM], ACT.Exp,
                                             bias=x_neg[:, t % 2, h:h + 1], accum_out=x_sum[:, t % 2, h:h + 1])
                e.then_inc(sx_exp, 1)

            def x_pT(t):
                if t == 4:
                    act.wait_ge(tile_done, G_PV + KT)
                act.wait_ge(sx_tr, t + 1)
                o = (t % 4) * P
                nc.scalar.activation(pTx[:, :, o:o + P], psS[t % 2][:].rearrange("p (b t) -> p b t", t=P), ACT.Copy).then_inc(sx_pT, 1)

            def x_out(half):
                for j in range(KT):
                    g = G_PV + half * KT + j
                    act.wait_ge(tile_done, g + 1)
                    nc.scalar.activation(act_hi[:, j, half * HALF:(half + 1) * HALF], psG[g % 2][:], ACT.Copy).then_inc(hi_out, 1)

            x_exp(0)
            x_exp(1)
            for t in range(TT):
                x_pT(t)
                if t % 4 == 3:
                    if t + 2 < TT:
                        x_exp(t + 2)
                    x_out(t // 4)
                elif t + 2 < TT:
                    x_exp(t + 2)
            for m in range(3, 8):
                if m == 3:
                    act.wait_ge(sx_tr, TT)
                block_hi(C_XO + m, m % 2, m)

            def extra_x(t):
                if t in (2, 3, 4, 5):
                    block_hi(C_MLP + t - 2, t % 2, t - 2)
            residual_norm_act(G_XO, N_X, extra_x)
            for t in range(2):
                norm_hi(N_X + TT - 2 + t, act_tile(TT - 2 + t))
            act.wait_ge(tile_done, G_MLP)
            for m in range(4, 8):
                block_hi(C_MLP + m, m % 2, m)

            def mlp_group(g, last):
                for c in range(4):
                    for half in range(2):
                        j = 2 * c + half
                        act.wait_ge(tile_done, g * MLP_TILES + (G_MLP + j + 1))
                        if not isinstance(g, int) or g or j >= 2:
                            pass
                        act.wait_ge(tile_out, g * MLP_TILES + (G_MLP + j - 1))
                        nc.scalar.activation(r_ff[:, half, :], psG[half][:], ACT.Relu).then_inc(relu_out, 1)
                        act.wait_ge(sq_out, g * 8 + (j + 1))
                        nc.scalar.activation(a_hi[:, c, half * HALF:(half + 1) * HALF], r_ff[:, half, :], ACT.Copy).then_inc(hi_out, 1)
                    if not last:
                        block_hi(None, c % 2, c, g * 64 + 16 * ((C_MLP + 8 + c) // 2 + 1))
                if not last:
                    act.wait_ge(tile_done, g * MLP_TILES + (G_MLP + MLP_TILES))
                    for c in range(4, 8):
                        block_hi(None, c % 2, c, g * 64 + 16 * ((C_MLP + 8 + c) // 2 + 1))

            with act.Fori(0, GROUPS - 1) as g:
                mlp_group(g, False)
            mlp_group(GROUPS - 1, True)
            for t in range(TT):
                n = N_F + t
                if t >= 2:
                    sq(n, X[:, t, :], f_hn[n % 2], (out_stored[n % 2], 16 * (t // 2)), (tile_out, G_MLP + (GROUPS - 1) * MLP_TILES + 8 + 2 * t + 2))
                else:
                    sq(n, X[:, t, :], f_hn[n % 2], (tile_out, G_MLP + (GROUPS - 1) * MLP_TILES + 8 + 2 * t + 2))
                root(n)

        @block.vector
        def _(dve):
            def lo_part(dst, src, hi, sem_):
                nc.vector.tensor_tensor(dst, src, hi.bitcast(f32), ALU.subtract).then_inc(sem_, 1)

            def norm_var(n):
                i = slice(n % 2, n % 2 + 1)
                dve.wait_ge(n_sq, n + 1)
                nc.vector.tensor_scalar(var[:, i], sum_sq[:, i], 1.0 / D, EPS, ALU.mult, ALU.add).then_inc(n_var, 1)

            def norm_scale(n, src, dst, gain_t, *waits):
                i = slice(n % 2, n % 2 + 1)
                dve.wait_ge(n_std, n + 1)
                nc.vector.reciprocal(rstd0[:, i], std[:, i]).then_inc(n_chain, 1)
                dve.wait_ge(n_chain, 4 * n + 1)
                nc.vector.scalar_tensor_tensor(newt[:, 0, i], rstd0[:, i], rstd0[:, i], var[:, i], ALU.mult, ALU.mult).then_inc(n_chain, 1)
                dve.wait_ge(n_chain, 4 * n + 2)
                nc.vector.tensor_scalar(newt[:, 1, i], newt[:, 0, i], -0.5, 1.5, ALU.mult, ALU.add).then_inc(n_chain, 1)
                dve.wait_ge(n_chain, 4 * n + 3)
                nc.vector.tensor_tensor(rstd[:, i], rstd0[:, i], newt[:, 1, i], ALU.mult).then_inc(n_chain, 1)
                dve.wait_ge(n_chain, 4 * n + 4)
                for s_, v in waits:
                    dve.wait_ge(s_, v)
                nc.vector.scalar_tensor_tensor(dst[:], src, rstd[:, i], gain_t[:], ALU.mult, ALU.mult).then_inc(n_hn, 1)

            def norm_lo(n, dst_lo, dst_hi):
                dve.wait_ge(n_hi, n + 1)
                lo_part(dst_lo, psS[n % 2][:].rearrange("p (k t) -> p k t", t=P), dst_hi, n_lo)

            def act_tile(a, t):
                return a[:, :, t * P:(t + 1) * P]

            def block_lo(n, slot, raw_slot):
                dve.wait_ge(hi_done, n + 1)
                lo_part(w_lo[slot][:], raw[raw_slot][:], w_hi[slot][:], lo_done)

            nc.vector.memset(gate_raw[:], 0.0).then_inc(gate_zeroed, 1)
            for a in range(2):
                for h in range(2):
                    nc.vector.memset(qA[a][h][HEAD:HEAD + 1, :], 1.0).then_inc(ones_set, 1)
            for t in range(TT):
                norm_var(t)
                if t >= 1:
                    norm_lo(t - 1, act_tile(act_lo, t - 1), act_tile(act_hi, t - 1))
                norm_scale(t, X[:, t, :], a_hn[t % 2], a_gain, (gain_loaded[0], 16))
                if t == 3:
                    for j in range(3):
                        block_lo(j, j, j)
            norm_lo(TT - 1, act_tile(act_lo, TT - 1), act_tile(act_hi, TT - 1))
            dve.wait_ge(gate_hi_done, 1)
            lo_part(gate_lo[:], gate_raw[:], gate_hi[:], gate_lo_done)

            def qkv_out(par, j):
                chunk, half = divmod(j, 2)
                tok = slice(half * HALF, (half + 1) * HALF)
                if chunk == 2:
                    nc.vector.tensor_copy(vT[:, tok], psG[half][:]).then_inc(tile_out, 1)
                    return
                for h in range(2):
                    src = psG[half][h * HEAD:(h + 1) * HEAD, :]
                    if chunk == 0:
                        e = nc.vector.tensor_scalar(qA[par][h][0:HEAD, tok], src, 1.0 / math.sqrt(HEAD), None, ALU.mult)
                    else:
                        e = nc.vector.tensor_copy(kA[par][h][0:HEAD, tok], src)
                e.then_inc(tile_out, 1)

            for j in range(6):
                dve.wait_ge(tile_done, j + 1)
                qkv_out(0, j)
                if j % 2 == 1:
                    block_lo(3 + j // 2, j // 2, j // 2)
            dve.wait_ge(gate_act, 3)
            dve.sem_inc(tile_out, 2)
            nc.vector.tensor_scalar(gate_z[:], gate_z[:], -1.0, 0.0, ALU.mult, ALU.max).then_inc(gate_dve, 1)
            dve.wait_ge(gate_dve, 1)
            dve.wait_ge(gate_act, 5)
            nc.vector.tensor_tensor(gate_z[:], gate_z[:], gate_e[:], ALU.add).then_inc(gate_dve, 1)
            dve.wait_ge(gate_dve, 2)
            nc.vector.tensor_tensor_scan(gate_l[:], gate_z[:], gate_z[:], 0.0, ALU.add, ALU.bypass).then_inc(gate_dve, 1)

            def max_step(u, value):
                n = (u % QB + 1) * P
                dve.wait_ge(qk_done, value)
                dve.sem_inc(max_gate, 1)
                nc.vector.tensor_tensor_reduce(out=S[u % 2][:, 0:n], in0=psS[u % 2][:, 0:n], in1=mask[:, T - n:T], scale=-1.0,
                                               scalar=3.0e38, op0=ALU.add, op1=ALU.min,
                                               accum_out=row_max[:, u % 2:u % 2 + 1]).then_inc(max_done, 1)

            dve.wait_ge(mask_loaded, 16)
            dve.wait_ge(cum_stored, 16)
            max_step(0, 1)

            def pair_dve(it, p, par, has_next, splits):
                for ev in dilated_steps(has_next):
                    kind, u = ev[0], ev[1]
                    h, qb = divmod(u % STEPS, QB)
                    if kind == "QK":
                        if u == STEPS and splits and par == 1:
                            dve.wait_ge(mask_loaded, it * 16 + 32)
                        max_step(u, p * 16 + (u + 1))
                    elif kind == "V":
                        dve.wait_ge(tile_done, body_tile(p, u))
                        nc.vector.tensor_copy(V[par][:, 4 * u:4 * u + 4, :],
                                              psG[u][:].rearrange("p (b d) -> p b d", d=P)).then_inc(tile_out, 1)
                    elif kind == "PV":
                        i = slice(u % 2, u % 2 + 1)
                        dve.wait_ge(exp_done, p * 16 + (u + 1))
                        nc.vector.reciprocal(row_inv[:, i], row_sum[:, i]).then_inc(inv_done, 1)
                        dve.wait_ge(inv_done, p * 16 + (u + 1))
                        dve.wait_ge(pv_done, p * 16 + (u + 1))
                        dst = X[:, qb, bass.ds(p * P + h * HEAD, HEAD)]
                        nc.vector.tensor_scalar(dst, psO[u % 2][:, 0:HEAD], row_inv[:, i], None,
                                                ALU.mult).then_inc(o_out, 1)
                    elif kind == "tile":
                        dve.wait_ge(tile_done, body_tile(p, u + 2))
                        qkv_out(1 - par, u)
                        if u % 2 == 1 and splits:
                            block_lo(p * 3 + (6 + u // 2), u // 2, u // 2)

            with dve.Fori(0, 3) as it:
                for par in range(2):
                    pair_dve(it, it * 2 + par, par, True, True)
            pair_dve(3, 6, 0, True, False)
            for m in range(3):
                block_lo(B_BLOCKS + C_OUT + m, m, m % 2)
            pair_dve(3, 7, 1, False, False)
            block_lo(B_BLOCKS + C_OUT + 3, 3, 1)

            def y_split(t):
                dve.wait_ge(y_hi, t + 1)
                lo_part(act_tile(act_lo, t), psS[t % 2][:].rearrange("p (k t) -> p k t", t=P), act_tile(act_hi, t), y_lo)

            def add_residual(g, t, half):
                dve.wait_ge(tile_done, g + 1)
                cs = slice(half * HALF, (half + 1) * HALF)
                nc.vector.tensor_tensor(X[:, t, cs], X[:, t, cs], psG[g % 2][:], ALU.add).then_inc(tile_out, 1)

            for t in range(TT):
                y_split(t)
                if t in (1, 2, 3, 4):
                    block_lo(B_BLOCKS + C_OUT + 3 + t, 3 + t, (3 + t) % 2)
                if t >= 1:
                    dve.wait_ge(x_loaded[t - 1], 32)
                    add_residual(G_OUT + t - 1, t - 1, 0)
            dve.wait_ge(x_loaded[TT - 1], 32)
            add_residual(G_OUT + TT - 1, TT - 1, 0)

            def residual_norm_dve(g0, n0, gain_t, gain_sem, extra):
                for t in range(TT):
                    n = n0 + t
                    add_residual(g0 + TT + t, t, 1)
                    norm_var(n)
                    if t >= 2:
                        norm_lo(n - 2, act_tile(act_lo, t - 2), act_tile(act_hi, t - 2))
                    norm_scale(n, X[:, t, :], c_hn[n % 2], gain_t, (gain_sem, 16))
                    extra(t)

            def extra_c(t):
                if t in (2, 3):
                    block_lo(B_BLOCKS + C_XK + t - 2, t - 2, t - 2)
            residual_norm_dve(G_OUT, N_C, c_gain, gain_loaded[1], extra_c)
            for t in range(MT):
                n = N_M + t
                norm_var(n)
                norm_lo(n - 2, act_tile(act_lo, TT - 2 + t), act_tile(act_hi, TT - 2 + t))
                norm_scale(n, m_in[:, t, :], c_hn[n % 2], m_gain, (gain_loaded[2], 16))
            for t in range(MT):
                norm_lo(N_M + t, mT_lo[:, :, t * P:(t + 1) * P], mT_hi[:, :, t * P:(t + 1) * P])

            with dve.Fori(0, 4) as c:
                for i in range(2):
                    dve.wait_ge(tile_done, c * 2 + (G_XK + i + 1))
                    nc.vector.tensor_copy(kx[:, bass.ds(c * 2 + i, 1), :].rearrange("p o n -> p (o n)"),
                                          psG[(G_XK + i) % 2][:, 0:N_MEM]).then_inc(tile_out, 1)
                    block_lo(c * 2 + (B_BLOCKS + C_XK + 2 + i), i, i)
            with dve.Fori(0, 4) as c:
                for i in range(2):
                    dve.wait_ge(tile_done, c * 4 + (G_XV + 2 * i + 1))
                    nc.vector.tensor_copy(vxT[:, i, :], psG[0][:, 0:N_MEM]).then_inc(tile_out, 1)
                    dve.wait_ge(tile_done, c * 4 + (G_XV + 2 * i + 2))
                    nc.vector.tensor_copy(vx[:, :, bass.ds(c * 256 + i * P, P)],
                                          psG[1][:, 0:N_MEM].rearrange("p (b d) -> p b d", d=P)).then_inc(tile_out, 1)
                    block_lo(c * 2 + (B_BLOCKS + C_XV + 2 + i), i, i)
            with dve.Fori(0, 4) as c:
                for i in range(2):
                    for half in range(2):
                        dve.wait_ge(tile_done, c * 4 + (G_XQ + 2 * i + half + 1))
                        nc.vector.tensor_scalar(qx[:, bass.ds(c * 2 + i, 1), half * HALF:(half + 1) * HALF].rearrange("p o n -> p (o n)"),
                                                psG[half][:], 1.0 / math.sqrt(D // X_HEADS), None, ALU.mult).then_inc(tile_out, 1)
                    block_lo(c * 2 + (B_BLOCKS + C_XQ + 2 + i), i, i)
            block_lo(B_BLOCKS + C_XO + 2, 2, 0)

            def x_row_max(t):
                dve.wait_ge(sx_done, t + 1)
                nc.vector.tensor_reduce(x_max[:, t % 2, :], psS[t % 2][:].rearrange("p (h n) -> p h n", n=N_MEM),
                                        AX.X, ALU.max).then_inc(sx_max, 1)
                dve.wait_ge(sx_max, t + 1)
                nc.vector.tensor_scalar(x_neg[:, t % 2, :], x_max[:, t % 2, :], -1.0, None, ALU.mult).then_inc(sx_neg, 1)

            def x_normalise(t):
                dve.wait_ge(sx_exp, t + 1)
                nc.vector.reciprocal(x_inv[:, t % 2, :], x_sum[:, t % 2, :]).then_inc(sx_inv, 1)
                dve.wait_ge(sx_inv, t + 1)
                nc.vector.tensor_tensor(Sx[t % 2][:], Sx[t % 2][:],
                                        x_inv[:, t % 2, :].rearrange("p (h o) -> p h o", o=1).to_broadcast([P, X_HEADS, N_MEM]),
                                        ALU.mult).then_inc(sx_norm, 1)

            def x_out_lo(half):
                for j in range(KT):
                    g = G_PV + half * KT + j
                    dve.wait_ge(hi_out, half * KT + j + 1)
                    cs = slice(half * HALF, (half + 1) * HALF)
                    lo_part(act_lo[:, j, cs], psG[g % 2][:], act_hi[:, j, cs], tile_out)

            x_row_max(0)
            x_row_max(1)
            for t in range(TT):
                x_normalise(t)
                if t + 2 < TT:
                    x_row_max(t + 2)
                if t % 4 == 3:
                    x_out_lo(t // 4)
            for m in range(3, 8):
                block_lo(B_BLOCKS + C_XO + m, m, m % 2)
            for t in range(TT):
                add_residual(G_XO + t, t, 0)

            def extra_x(t):
                if t in (2, 3, 4, 5):
                    block_lo(B_BLOCKS + C_MLP + t - 2, t - 2, t % 2)
            residual_norm_dve(G_XO, N_X, c_gain, gain_loaded[3], extra_x)
            for t in range(TT - 2, TT):
                norm_lo(N_X + t, act_tile(act_lo, t), act_tile(act_hi, t))
            for m in range(4, 8):
                block_lo(B_BLOCKS + C_MLP + m, m, m % 2)

            def mlp_group(g, last):
                for c in range(4):
                    for half in range(2):
                        j = 2 * c + half
                        cs = slice(half * HALF, (half + 1) * HALF)
                        dve.wait_ge(relu_out, g * 8 + (j + 1))
                        nc.vector.tensor_tensor(r_ff[:, half, :], r_ff[:, half, :], r_ff[:, half, :], ALU.mult).then_inc(sq_out, 1)
                        dve.wait_ge(hi_out, g * 8 + (2 * KT + j + 1))
                        lo_part(a_lo[:, c, cs], r_ff[:, half, :], a_hi[:, c, cs], tile_out)
                    if not last:
                        block_lo(g * 8 + (B_BLOCKS + C_MLP + 8 + c), c, c % 2)
                for t in range(TT):
                    for half in range(2):
                        dve.wait_ge(tile_done, g * MLP_TILES + (G_MLP + 8 + 2 * t + half + 1))
                        cs = slice(half * HALF, (half + 1) * HALF)
                        nc.vector.tensor_tensor(X[:, t, cs], X[:, t, cs], psG[half][:], ALU.add).then_inc(tile_out, 1)
                if not last:
                    for c in range(4, 8):
                        block_lo(g * 8 + (B_BLOCKS + C_MLP + 8 + c), c, c % 2)

            with dve.Fori(0, GROUPS - 1) as g:
                mlp_group(g, False)
            mlp_group(GROUPS - 1, True)
            for t in range(TT):
                n = N_F + t
                norm_var(n)
                norm_scale(n, X[:, t, :], f_hn[n % 2], f_gain, (gain_loaded[4], 16))


_INS = ["x", "mem", "g_mix", "w_in", "b_forget", "w_out", "g_xattn", "g_mem", "w_xq", "w_xk", "w_xv", "w_xo",
        "g_mlp", "w_up", "w_down", "g_final"]


def _shape_constants():
    ident = np.eye(P, dtype=np.float32)
    delta = (T - P) + np.arange(P)[:, None] - np.arange(T)[None, :]
    times = sum(((delta >= 0) & (delta <= w) & (delta % d == 0)).astype(np.int64) for w, d in DILATIONS)
    dilated = np.where(times > 0, np.log(np.maximum(times, 1)), NEG).astype(np.float32)
    causal = np.where(delta >= 0, 0.0, NEG).astype(np.float32)
    slopes = 2.0 ** -np.arange(1, 9, dtype=np.float64)
    alibi = (slopes[:, None] * np.arange(T)[None, :]).astype(np.float32)
    return {"ident": ident, "masks": np.stack([dilated, dilated, causal, causal]), "alibi": alibi}


def kernel(**inputs):
    import concourse.bacc as _bacc
    from concourse.bass_utils import run_bass_kernel_spmd as _run

    nc = _bacc.Bacc("TRN2", target_bir_lowering=False, num_devices=1)
    arrays, args = {}, []
    for name in _INS:
        a = np.ascontiguousarray(inputs[name])
        arrays[f"in_{name}_dram"] = a
        args.append(nc.dram_tensor(f"in_{name}_dram", a.shape, mybir.dt.from_np(a.dtype), kind="ExternalInput").ap())
    for name, a in _shape_constants().items():
        arrays[f"const_{name}_dram"] = a
        args.append(nc.dram_tensor(f"const_{name}_dram", a.shape, mybir.dt.from_np(a.dtype), kind="ExternalInput").ap())
    args.append(nc.dram_tensor("out_0_dram", (1, T, D), mybir.dt.float32, kind="ExternalOutput").ap())
    hybrid_layer(nc, *args)
    r = _run(nc, [arrays], core_ids=[0])
    return r.results[0]["out_0_dram"]
```

```python
import math
from contextlib import ExitStack

import numpy as np

import concourse.bass as bass
from concourse import mybir

P = 128
T = 1024
D = 1024
KT = D // P
TT = T // P
HALF = 512
N_MEM = 256
MT = N_MEM // P
HEAD = 64
PAIRS = 8
STEPS = 16
QB = T // P
X_HEADS = 4
D_FF = 4096
GROUPS = D_FF // HALF
EPS = 1e-6
NEG = -1e30
DILATIONS = ((128, 1), (512, 4), (2048, 16))
GATE_COL = 6 * PAIRS // 2 * P
KB = 1024


V_, Q_, K_, GATE_ = range(4)
PAIR_TILES = ((V_, 0), (V_, 1), (Q_, 0), (K_, 0), (Q_, 1), (K_, 1))
FIRST_TILES = ((V_, 0), (Q_, 0), (K_, 0), (GATE_, 0), (GATE_, 1), (V_, 1), (Q_, 1), (K_, 1))
PRODUCTS = 3 * KT


def gaps():
    room = []
    for u in range(STEPS):
        n, n1 = u % QB + 1, (u + 1) % QB + 1
        first = max(0.2, 0.9 + 0.11 * n - 0.11 * n1)
        room += [first, max(0.2, 1.4 + 0.25 * n1 - 0.11 * n - first)]
    return room


def pair_steps(has_next):
    room = gaps()
    total = PRODUCTS * len(PAIR_TILES) if has_next else 0
    order = []
    done = 0
    for u in range(STEPS):
        order.append(("T", u))
        if u in VT_STEPS and has_next:
            order.append(("VT", VT_STEPS.index(u)))
        if u + 1 < STEPS or has_next:
            order.append(("QK", u + 1))
        if u == 0:
            order.append(("last", len(PAIR_TILES) - 1))
        for part in range(2):
            upto = round(total * sum(room[:2 * u + part + 1]) / sum(room))
            while done < upto:
                j, r0 = divmod(done, PRODUCTS)
                r1 = min(PRODUCTS, r0 + upto - done)
                order.append(("G", j, r0, r1))
                if r1 == PRODUCTS:
                    order.append(("tile", j))
                done += r1 - r0
            if part == 0:
                order.append(("PV", u))
    return order


VT_STEPS = (8, 9)


def hybrid_layer(nc, x, mem, g_mix, w_in, b_forget, w_out, g_xattn, g_mem, w_xq, w_xk, w_xv, w_xo,
                 g_mlp, w_up, w_down, g_final, ident_c, masks_c, bias_c, out):
    f32, f32r = mybir.dt.float32, mybir.dt.float32r
    ALU, ACT, AX = mybir.AluOpType, mybir.ActivationFunctionType, mybir.AxisListType

    x_t = x[0].rearrange("(t p) d -> t p d", p=P)
    out_t = out[0].rearrange("(t p) d -> t p d", p=P)
    mem_t = mem[0].rearrange("(t p) d -> t p d", p=P)

    def k_rows(w):
        return w.rearrange("(k p) n -> p k n", p=P)

    w_in_k, w_out_k, w_xq_k, w_xk_k, w_xv_k, w_xo_k, w_up_k = map(
        k_rows, (w_in, w_out, w_xq, w_xk, w_xv, w_xo, w_up))
    bias_rows = nc.dram_tensor("bias_rows", (2 * PAIRS, 8, T), f32).ap()

    base = 16 * KB + 512

    def at(name, shape, dt, kb):
        return nc.alloc_sbuf_tensor_at(name, shape, dt, offset=base + int(kb * KB))

    act_hi = at("act_hi", [P, KT, T], f32r, 0)
    act_lo = at("act_lo", [P, KT, T], f32r, 32)
    X = at("X", [P, TT, D], f32, 64)
    ident = at("ident", [P, P], f32, 96)
    row_max = at("row_max", [P, 2], f32, 96.5)
    row_sum = at("row_sum", [P, 2], f32, 96.5625)
    sum_sq = at("sum_sq", [P, 2], f32, 96.625)
    var = at("var", [P, 2], f32, 96.6875)
    std = at("std", [P, 2], f32, 96.75)
    rstd0 = at("rstd0", [P, 2], f32, 96.8125)
    newt = at("newt", [P, 2, 2], f32, 96.875)
    rstd = at("rstd", [P, 2], f32, 96.9375)
    x_max = at("x_max", [P, 2, X_HEADS], f32, 97)
    x_neg = at("x_neg", [P, 2, X_HEADS], f32, 97.0625)
    x_sum = at("x_sum", [P, 2, X_HEADS], f32, 97.125)
    x_inv = at("x_inv", [P, 2, X_HEADS], f32, 97.1875)
    b_col = at("b_col", [8, 1], f32, 97.25)
    row_inv = at("row_inv", [P, 2], f32, 97.3125)
    slot_kb = [98, 106, 114, 134, 142, 150, 158, 166]
    w_hi = [at(f"w_hi{i}", [P, 1024], f32r, kb) for i, kb in enumerate(slot_kb)]
    w_lo = [at(f"w_lo{i}", [P, 1024], f32r, kb + 4) for i, kb in enumerate(slot_kb)]
    raw = [at(f"raw{i}", [P, 1024], f32, 122 + 4 * i) for i in range(2)]
    sets = [[134 + 32 * a + 16 * h for h in range(2)] for a in range(2)]
    qhl = [[at(f"qhl{a}{h}", [P, T], f32r, sets[a][h]) for h in range(2)] for a in range(2)]
    khh = [[at(f"khh{a}{h}", [P, T], f32r, sets[a][h] + 4) for h in range(2)] for a in range(2)]
    qb_ = [[at(f"qb{a}{h}", [HEAD + 4, T], f32r, sets[a][h] + 8) for h in range(2)] for a in range(2)]
    klb = [[at(f"klb{a}{h}", [HEAD + 4, T], f32r, sets[a][h] + 12) for h in range(2)] for a in range(2)]
    V = [at(f"V{a}", [P, TT, P], f32, 198 + 4 * a) for a in range(2)]
    vT = at("vT", [P, T], f32, 114)
    S = at("S", [P, T], f32, 118)
    pT = at("pT", [P, T], f32, 126)
    mask = at("mask", [P, T], f32, 130)
    first_k = (at("first_k_hi", [P, 1024], f32r, 118), at("first_k_lo", [P, 1024], f32r, 126))
    gate_raw = at("gate_raw", [P, 1024], f32, 178)
    gate_hi = at("gate_hi", [P, 1024], f32r, 182)
    gate_lo = at("gate_lo", [P, 1024], f32r, 186)
    gate_z = at("gate_z", [8, T], f32, 190)
    gate_e = at("gate_e", [8, T], f32, 194)
    cum = at("cum", [8, T], f32, 202)
    cum_hi = at("cum_hi", [8, T], f32r, 166)
    cum_lo = at("cum_lo", [8, T], f32r, 170)
    a_hn = [at(f"a_hn{i}", [P, D], f32, 166 + 4 * i) for i in range(2)]
    a_gain = at("a_gain", [P, D], f32, 174)
    c_hn = [at(f"c_hn{i}", [P, D], f32, 174 + 4 * i) for i in range(2)]
    c_gain = at("c_gain", [P, D], f32, 182)
    x_hn = [at(f"x_hn{i}", [P, D], f32, kb) for i, kb in enumerate((186, 202))]
    x_gain = at("x_gain", [P, D], f32, 198)
    m_gain = at("m_gain", [P, D], f32, 186)
    m_in = at("m_in", [P, D], f32, 130)
    mT_hi = at("mT_hi", [P, KT, N_MEM], f32r, 190)
    mT_lo = at("mT_lo", [P, KT, N_MEM], f32r, 198)
    kx = at("kx", [P, KT, N_MEM], f32, 150)
    vx = at("vx", [P, MT, D], f32, 98)
    vxT = at("vxT", [P, 2, N_MEM], f32, 130)
    qx = at("qx", [P, KT, T], f32, 158)
    Sx = [at(f"Sx{i}", [P, X_HEADS, N_MEM], f32, 106 + 4 * i) for i in range(2)]
    pTx = at("pTx", [P, 2 * X_HEADS, HALF], f32, 190)
    r_ff = at("r_ff", [P, 2, HALF], f32, 130)
    a_hi = at("a_hi", [P, 4, T], f32r, 174)
    a_lo = at("a_lo", [P, 4, T], f32r, 190)
    f_hn = [at(f"f_hn{i}", [P, D], f32, 106 + 4 * i) for i in range(2)]
    f_gain = at("f_gain", [P, D], f32, 114)

    with ExitStack() as ctx:
        def sem(name):
            return ctx.enter_context(nc.semaphore(name))

        psS = [ctx.enter_context(nc.psum_tensor(f"psS{i}", [P, 1024], f32)) for i in range(2)]
        psG = [ctx.enter_context(nc.psum_tensor(f"psG{i}", [P, HALF], f32)) for i in range(2)]
        psO = ctx.enter_context(nc.psum_tensor("psO", [P, 2, HALF], f32))

        consts_loaded = sem("consts_loaded")
        b_loaded = sem("b_loaded")
        bias_stored = sem("bias_stored")
        gain_loaded = [sem(f"gain_loaded{i}") for i in range(5)]
        x_loaded = [sem(f"x_loaded{i}") for i in range(TT)]
        m_loaded = [sem(f"m_loaded{i}") for i in range(MT)]
        rawB = sem("rawB_loaded")
        rawC = [sem(f"rawC_loaded{i}") for i in range(2)]
        gate_zeroed = sem("gate_zeroed")
        gate_loaded = sem("gate_loaded")
        gate_hi_done = sem("gate_hi_done")
        gate_lo_done = sem("gate_lo_done")
        gate_act = sem("gate_act")
        gate_dve = sem("gate_dve")
        cum_stored = sem("cum_stored")
        bias_loaded = [sem(f"bias_loaded{i}") for i in range(2)]
        mask_loaded = sem("mask_loaded")
        hi_done = sem("hi_done")
        lo_done = sem("lo_done")
        tile_done = sem("tile_done")
        tile_out = sem("tile_out")
        qk_done = sem("qk_done")
        vt_done = sem("vt_done")
        vt_out = sem("vt_out")
        qk_hi = sem("qk_hi")
        raw_gate = sem("raw_gate")
        max_gate = sem("max_gate")
        max_done = sem("max_done")
        exp_done = sem("exp_done")
        inv_done = sem("inv_done")
        tr_done = sem("tr_done")
        pT_done = sem("pT_done")
        pv_done = sem("pv_done")
        o_out = sem("o_out")
        yt_done = sem("yt_done")
        y_hi = sem("y_hi")
        y_lo = sem("y_lo")
        n_sq = sem("n_sq")
        n_var = sem("n_var")
        n_std = sem("n_std")
        n_chain = sem("n_chain")
        n_hn = sem("n_hn")
        n_tr = sem("n_tr")
        n_hi = sem("n_hi")
        n_lo = sem("n_lo")
        sx_done = sem("sx_done")
        sx_max = sem("sx_max")
        sx_neg = sem("sx_neg")
        sx_exp = sem("sx_exp")
        sx_inv = sem("sx_inv")
        sx_norm = sem("sx_norm")
        sx_tr = sem("sx_tr")
        sx_pT = sem("sx_pT")
        hi_out = sem("hi_out")
        relu_out = sem("relu_out")
        sq_out = sem("sq_out")
        out_stored = [sem(f"out_stored{i}") for i in range(2)]

        PRO_TILES = len(FIRST_TILES)
        B_TILES = PRO_TILES + 7 * len(PAIR_TILES)
        QK_COUNT = {j: n + 1 for n, j in enumerate(j for j, (chunk, _) in enumerate(PAIR_TILES) if chunk != V_)}
        LAST = len(PAIR_TILES) - 1
        SPLIT_AT = {("T", 2): 1, ("tile", 1): 2, ("tile", 4): 3}
        B_BLOCKS = 3 * PAIRS

        def body_tile(p, j):
            return p * len(PAIR_TILES) + (PRO_TILES + j + 1)

        def pair_slot(par, chunk):
            return (3 * (1 - par) + chunk) % 2

        OUT_SLOTS = (3, 4, 5, 6, 0, 1, 2, 7)
        XO_SLOTS = (3, 4, 2, 1, 0, 5, 6, 7)
        X_SLOTS = (3, 4)
        MLP_SLOTS = XO_SLOTS

        OUT_STEPS = (1, 4, 7, 11)

        def raw_of(m):
            if m < 8:
                i = (0, 0, 0, 0, 1, 0, 1, 0)[m]
                return i, (1, 2, 3, 4, 1, 5, 2, 6)[m]
            return m % 2, m // 2 + (3 if m % 2 == 0 else -1)

        N_M, N_C, N_X, N_F = TT, TT + MT, 2 * TT + MT, 3 * TT + MT
        C_OUT, C_XK, C_XV, C_XQ, C_XO, C_MLP = 0, 8, 16, 24, 32, 40
        G_OUT = B_TILES
        G_XK = G_OUT + 2 * TT
        G_XV = G_XK + KT
        G_XQ = G_XV + 2 * KT
        G_PV = G_XQ + 2 * KT
        G_XO = G_PV + 2 * KT
        G_MLP = G_XO + 2 * TT
        MLP_TILES = 8 + 2 * TT

        block = ctx.enter_context(nc.Block())

        def pair_cols(w, p, j):
            c = (p // 4) * 3 * HALF + {V_: 2, Q_: 0, K_: 1}[j] * HALF + (p % 4) * P
            return w[:, :, c:c + P]

        @block.sync
        def _(sp):
            def gain(i, dst, g):
                sp.dma_start(dst[:], g.rearrange("(a d) -> a d", a=1).to_broadcast([P, D])).then_inc(gain_loaded[i], 16)

            def raw_pair(p, j, col=None):
                src = w_in_k[:, :, bass.ds(col, P)] if col is not None else pair_cols(w_in_k, p, j)
                if not isinstance(p, int) or 3 * p + j:
                    sp.wait_ge(lo_done, p * 3 + j)
                    sp.sem_inc(raw_gate, 1)
                sp.dma_start(raw[0][:].rearrange("p (k n) -> p k n", n=P), src).then_inc(rawB, 16)

            def bias(heads, par):
                for h, head in enumerate(heads):
                    for side, dst in ((0, qb_), (1, klb)):
                        rows4 = bias_rows[bass.ds(head, 1), 4 * side:4 * side + 4, :].rearrange("o r n -> (o r) n")
                        sp.dma_start(dst[par][h][HEAD:HEAD + 4, :].bitcast(f32), rows4).then_inc(bias_loaded[par], 16)

            def raw_block(m, i, src, shape):
                sp.wait_ge(lo_done, m + (B_BLOCKS - 1))
                sp.dma_start(shape(raw[i]), src).then_inc(rawC[i], 16)

            for t in range(TT):
                if t == 1:
                    gain(0, a_gain, g_mix)
                    sp.dma_start(ident[:], ident_c).then_inc(consts_loaded, 16)
                sp.dma_start(X[:, t, :], x_t[t]).then_inc(x_loaded[t], 16)
                if t == 3:
                    raw_pair(0, 0)
            sp.dma_start(b_col[:], b_forget.rearrange("(h a) -> h a", a=1)).then_inc(b_loaded, 16)
            sp.wait_ge(gate_zeroed, 1)
            sp.dma_start(gate_raw[:].rearrange("p (k n) -> p k n", n=P)[:, :, 0:8],
                         w_in_k[:, :, GATE_COL:GATE_COL + 8]).then_inc(gate_loaded, 16)
            raw_pair(0, 1)
            sp.dma_start(bias_rows, bias_c).then_inc(bias_stored, 16)
            raw_pair(0, 2)
            sp.dma_start(mask[:], masks_c[0]).then_inc(mask_loaded, 16)
            sp.wait_ge(bias_stored, 16)
            bias((0, 1), 0)
            for j in range(2):
                raw_pair(1, j)
            sp.wait_ge(gate_dve, 7)
            for r, src in ((4, cum_hi[:].bitcast(f32)), (5, cum_lo[:].bitcast(f32)), (2, gate_z[:]), (3, gate_e[:])):
                sp.dma_start(bias_rows[PAIRS:2 * PAIRS, r, :], src).then_inc(cum_stored, 16)
            sp.wait_ge(cum_stored, 64)

            def pair_loads(it, p, par):
                static = isinstance(p, int)
                k_col, next_col = (None, None) if static else (
                    sp.snap(((p + 1) // 4) * 1024 + (p + 1) * P + HALF), sp.snap(((p + 2) // 4) * 1024 + (p + 2) * P))
                heads = [2 * p + 2 + h if static else sp.snap(p * 2 + 2 + h) for h in range(2)]
                v_col = None if static else sp.snap(next_col + 2 * HALF)
                turn = None if static else sp.snap(it + 1)
                sp.wait_ge(qk_done, p * 16 + 1)
                bias(heads, 1 - par)
                raw_pair(p + 1, K_, k_col)
                if not static:
                    raw_pair(p + 2, V_, v_col)
                    raw_pair(p + 2, Q_, ((p + 2) // 4) * 1024 + (p + 2) * P)
                    if par == 1:
                        sp.wait_ge(max_done, p * 16 + 16)
                        sp.dma_start(mask[:], masks_c[bass.ds(turn, 1), :, :].rearrange("o p n -> (o p) n")).then_inc(mask_loaded, 16)

            with sp.Fori(0, 3) as it:
                for par in range(2):
                    pair_loads(it, it * 2 + par, par)
            pair_loads(3, 6, 0)
            def two_rows(w, half, i):
                return w[:, 2 * i:2 * i + 2, half * HALF:(half + 1) * HALF]

            def rows(r):
                return r[:].rearrange("p (k n) -> p k n", n=HALF)

            def cols(r):
                return r[:].rearrange("p (k n) -> p k n", n=P)

            def out_block(m):
                if m == 4:
                    sp.wait_ge(pv_done, PAIRS * STEPS)
                else:
                    before = max([n for n in range(m) if raw_of(n)[0] == raw_of(m)[0]], default=-1)
                    sp.wait_ge(lo_done, B_BLOCKS + before + 1)
                sp.dma_start(rows(raw[raw_of(m)[0]]), two_rows(w_out_k, m // 4, m % 4)).then_inc(rawC[raw_of(m)[0]], 16)

            for m in range(6):
                out_block(m)
            for t in range(TT):
                sp.wait_ge(yt_done, t + 1)
                sp.dma_start(X[:, t, :], x_t[t]).then_inc(x_loaded[t], 16)
                if t in (1, 2):
                    out_block(5 + t)
                if t == 3:
                    gain(2, m_gain, g_mem)
                    sp.dma_start(m_in[:], mem_t[0]).then_inc(m_loaded[0], 16)
            gain(1, c_gain, g_xattn)
            sp.wait_ge(n_hn, N_M + 1)
            sp.dma_start(m_in[:], mem_t[1]).then_inc(m_loaded[1], 16)
            for first, w in ((C_XK, w_xk_k), (C_XV, w_xv_k), (C_XQ, w_xq_k)):
                with sp.Fori(0, 4) as c:
                    for i in range(2):
                        raw_block(c * 2 + (first + i), i, w[:, :, bass.ds(c * 256 + i * P, P)], cols)
            for m in range(8):
                raw_block(C_XO + m, m % 2, two_rows(w_xo_k, m // 4, m % 4), rows)
                if m == 3:
                    sp.wait_ge(tile_done, G_PV + 2 * KT)
                    gain(3, x_gain, g_mlp)
            with sp.Fori(0, GROUPS) as g:
                for i in range(8):
                    if i < 4:
                        raw_block(g * 8 + (C_MLP + i), i % 2, w_up_k[:, :, bass.ds(g * HALF + i * P, P)], cols)
                    else:
                        raw_block(g * 8 + (C_MLP + i), i % 2, w_down[bass.ds(g * HALF + (i - 4) * P, P), :], lambda r: r[:])
            sp.wait_ge(tile_done, G_MLP + (GROUPS - 1) * MLP_TILES + 8)
            gain(4, f_gain, g_final)
            for t in range(TT):
                sp.wait_ge(n_hn, N_F + t + 1)
                sp.dma_start(out_t[t], f_hn[t % 2][:]).then_inc(out_stored[t % 2], 16)
            for i in range(2):
                sp.wait_ge(out_stored[i], 16 * TT // 2)

        @block.tensor
        def _(pe):
            def split_products(dst, parts, last_inc=None):
                n = len(parts)
                for k, (sh, sl, mh, ml) in enumerate(parts):
                    nc.tensor.matmul(dst, sh, mh, start=(k == 0), stop=False)
                    nc.tensor.matmul(dst, sh, ml, start=False, stop=False)
                    mm = nc.tensor.matmul(dst, sl, mh, start=False, stop=(k == n - 1))
                return mm

            def col_block(slot_hi, slot_lo, k):
                return slot_hi[:, k * P:(k + 1) * P], slot_lo[:, k * P:(k + 1) * P]

            def proj(j, chunk, half, r0, r1, slots):
                for r in range(r0, r1):
                    k, part = divmod(r, 3)
                    hi, lo = col_block(*slots[chunk], k)
                    mh = act_hi[:, k, half * HALF:(half + 1) * HALF]
                    ml = act_lo[:, k, half * HALF:(half + 1) * HALF]
                    a, b = ((hi, mh), (hi, ml), (lo, mh))[part]
                    mm = nc.tensor.matmul(psG[j % 2][:], a, b, start=(r == 0), stop=(r == 23))
                    if r == 23:
                        mm.then_inc(tile_done, 1)

            def scores(par, h, qb, u):
                n = (qb + 1) * P
                rows_q = slice(qb * P, (qb + 1) * P)
                for c in range(0, n, HALF):
                    dst = psS[u % 2][:, c:min(n, c + HALF)]
                    keys = slice(c, min(n, c + HALF))
                    nc.tensor.matmul(dst, qhl[par][h][:, rows_q], khh[par][h][:, keys], start=True, stop=False)
                    mm = nc.tensor.matmul(dst, qb_[par][h][:, rows_q], klb[par][h][:, keys], start=False, stop=True)
                mm.then_inc(qk_done, 1)

            def v_transposes(i):
                for b in range(4):
                    c = (4 * i + b) * P
                    mm = nc.tensor.transpose(psS[i][:, HALF + b * P:HALF + (b + 1) * P], vT[:, c:c + P], ident[:])
                mm.then_inc(vt_done, 1)

            def norm_tr(n, src):
                pe.wait_ge(n_hn, n + 1)
                if n >= 2:
                    pe.wait_ge(n_lo, n - 1)
                for k in range(KT):
                    mm = nc.tensor.transpose(psS[n % 2][:, k * P:(k + 1) * P], src[:, k * P:(k + 1) * P], ident[:])
                mm.then_inc(n_tr, 1)

            pe.wait_ge(consts_loaded, 16)
            for t in range(TT // 2):
                norm_tr(t, a_hn[t % 2])
            slots = [(w_hi[0], w_lo[0]), (w_hi[1], w_lo[1]), first_k, (gate_hi, gate_lo)]
            for j, (chunk, half) in enumerate(FIRST_TILES):
                if j == 0:
                    pe.wait_ge(n_lo, TT // 2)
                if j == 4:
                    pe.wait_ge(n_lo, TT)
                if j < 3:
                    pe.wait_ge(lo_done, j + 1)
                if j == 3:
                    pe.wait_ge(gate_lo_done, 1)
                if j >= 2:
                    pe.wait_ge(tile_out, j - 1)
                proj(j, chunk, half, 0, PRODUCTS, slots)
                if j < 2:
                    norm_tr(TT // 2 + 2 * j, a_hn[0])
                    norm_tr(TT // 2 + 2 * j + 1, a_hn[1])
            for i in range(2):
                v_transposes(i)
            pe.wait_ge(bias_loaded[0], 64)
            pe.wait_ge(tile_out, PRO_TILES - 1)
            scores(0, 0, 0, 0)

            def pair_pe(p, par, has_next):
                for ev in pair_steps(has_next):
                    kind, u = ev[0], ev[1]
                    h, qb = divmod(u % STEPS, QB)
                    if kind == "T":
                        pe.wait_ge(exp_done, p * 16 + (u + 1))
                        for b in range(qb + 1):
                            mm = nc.tensor.transpose(psS[u % 2][:, b * P:(b + 1) * P], S[:, b * P:(b + 1) * P], ident[:])
                        mm.then_inc(tr_done, 1)
                    elif kind == "QK":
                        if u >= 2:
                            pe.wait_ge(pT_done, p * 16 + (u - 1))
                        if u == STEPS:
                            pe.wait_ge(tile_out, body_tile(p, 3))
                            pe.wait_ge(bias_loaded[1 - par], bias_count(p, par))
                            scores(1 - par, 0, 0, u)
                        else:
                            if u == QB // 2:
                                pe.wait_ge(tile_out, body_tile(p, -1))
                                pe.wait_ge(vt_out, p * 2 + 2)
                            elif u == QB + QB // 2 and has_next:
                                pe.wait_ge(vt_out, p * 2 + 4)
                            scores(par, h, qb, u)
                    elif kind == "VT":
                        pe.wait_ge(tile_out, body_tile(p, 1))
                        v_transposes(u)
                    elif kind == "G":
                        j, r0, r1 = ev[1:]
                        chunk, half = PAIR_TILES[j]
                        if r0 == 0:
                            pe.wait_ge(tile_out, body_tile(p, j - 2))
                            if half == 0:
                                pe.wait_ge(lo_done, p * 3 + (3 + chunk + 1))
                        slot = pair_slot(par, chunk)
                        proj(j, 0, half, r0, r1, [(w_hi[slot], w_lo[slot])])
                    elif kind == "PV":
                        if u == 0:
                            pe.wait_ge(vt_out, p * 2 + 2)
                        pe.wait_ge(pT_done, p * 16 + (u + 1))
                        if u >= 2:
                            pe.wait_ge(o_out, p * 16 + (u - 1))
                        for b in range(qb + 1):
                            mm = nc.tensor.matmul(psO[:, u % 2, 0:HEAD], pT[:, b * P:(b + 1) * P],
                                                  V[par][:, b, h * HEAD:(h + 1) * HEAD], start=(b == 0), stop=(b == qb))
                        mm.then_inc(pv_done, 1)

            def bias_count(p, par):
                if isinstance(p, int):
                    return 64 * ((p + 1) // 2 + 1)
                return (p + (2 + par)) * 32

            with pe.Fori(0, 3) as it:
                for par in range(2):
                    pair_pe(it * 2 + par, par, True)
            pair_pe(6, 0, True)
            pair_pe(7, 1, False)

            def token_tile(psum, t, slots4):
                parts = []
                for k in range(KT):
                    i = slots4[k // 2]
                    cs = slice((k % 2) * HALF, (k % 2 + 1) * HALF)
                    tok = slice(t * P, (t + 1) * P)
                    parts.append((act_hi[:, k, tok], act_lo[:, k, tok], w_hi[i][:, cs], w_lo[i][:, cs]))
                return split_products(psum[:], parts)

            def residual_product(g0, block0, w_slots, n0, hn, before):
                for half in range(2):
                    for t in range(TT):
                        g = g0 + half * TT + t
                        before(half, t)
                        if t == 0:
                            pe.wait_ge(lo_done, B_BLOCKS + block0 + 4 * half + 4)
                        pe.wait_ge(tile_out, g - 1)
                        token_tile(psG[g % 2], t, w_slots[4 * half:4 * half + 4]).then_inc(tile_done, 1)
                        if half and t >= 2:
                            norm_tr(n0 + t - 2, hn[(n0 + t) % 2])

            def y_transposes(t):
                pe.wait_ge(o_out, PAIRS * STEPS)
                pe.wait_ge(pT_done, PAIRS * STEPS)
                if t >= 2:
                    pe.wait_ge(y_lo, t - 1)
                for k in range(KT):
                    mm = nc.tensor.transpose(psS[t % 2][:, k * P:(k + 1) * P], X[:, t, k * P:(k + 1) * P], ident[:])
                mm.then_inc(yt_done, 1)

            def before_out(half, t):
                if half == 0:
                    if t == 0:
                        y_transposes(0)
                    if t + 1 < TT:
                        y_transposes(t + 1)
                    pe.wait_ge(y_lo, t + 1)
                elif t < MT:
                    pe.wait_ge(y_lo, TT)
                    norm_tr(N_M + t, c_hn[t % 2])

            def last_norm_trs(n0, hn):
                for t in (TT - 2, TT - 1):
                    norm_tr(n0 + t, hn[(n0 + t) % 2])

            residual_product(G_OUT, C_OUT, OUT_SLOTS, N_C, c_hn, before_out)

            def mem_chunk(g, slot):
                return split_products(psG[g % 2][:, 0:N_MEM],
                                      [(*col_block(w_hi[slot], w_lo[slot], k), mT_hi[:, k, :], mT_lo[:, k, :]) for k in range(KT)])

            pe.wait_ge(n_lo, N_M + MT)
            with pe.Fori(0, 4) as c:
                for i in range(2):
                    pe.wait_ge(lo_done, c * 2 + (B_BLOCKS + C_XK + i + 1))
                    pe.wait_ge(tile_out, c * 2 + (G_XK + i - 1))
                    mem_chunk(G_XK + i, X_SLOTS[i]).then_inc(tile_done, 1)
            last_norm_trs(N_C, c_hn)

            with pe.Fori(0, 4) as c:
                for i in range(2):
                    pe.wait_ge(lo_done, c * 2 + (B_BLOCKS + C_XV + i + 1))
                    pe.wait_ge(tile_out, c * 4 + (G_XV + 2 * i - 1))
                    mem_chunk(G_XV, X_SLOTS[i]).then_inc(tile_done, 1)
                    pe.wait_ge(tile_out, c * 4 + (G_XV + 2 * i + 1))
                    for b in range(MT):
                        mm = nc.tensor.transpose(psG[1][:, b * P:(b + 1) * P], vxT[:, i, b * P:(b + 1) * P], ident[:])
                    mm.then_inc(tile_done, 1)

            pe.wait_ge(n_lo, N_C + TT)
            with pe.Fori(0, 4) as c:
                for i in range(2):
                    pe.wait_ge(lo_done, c * 2 + (B_BLOCKS + C_XQ + i + 1))
                    for half in range(2):
                        pe.wait_ge(tile_out, c * 4 + (G_XQ + 2 * i + half - 1))
                        tok = slice(half * HALF, (half + 1) * HALF)
                        split_products(psG[half][:], [(*col_block(w_hi[X_SLOTS[i]], w_lo[X_SLOTS[i]], k), act_hi[:, k, tok], act_lo[:, k, tok])
                                                      for k in range(KT)]).then_inc(tile_done, 1)

            def x_scores(t):
                if t >= 2:
                    pe.wait_ge(sx_pT, t - 1)
                for h in range(X_HEADS):
                    for c in range(2):
                        mm = nc.tensor.matmul(psS[t % 2][:, h * N_MEM:(h + 1) * N_MEM], qx[:, 2 * h + c, t * P:(t + 1) * P],
                                              kx[:, 2 * h + c, :], start=(c == 0), stop=(c == 1))
                mm.then_inc(sx_done, 1)

            def x_transposes(t):
                pe.wait_ge(sx_norm, t + 1)
                for b in range(2 * X_HEADS):
                    h, c = divmod(b, 2)
                    mm = nc.tensor.transpose(psS[t % 2][:, b * P:(b + 1) * P], Sx[t % 2][:, h, c * P:(c + 1) * P], ident[:])
                mm.then_inc(sx_tr, 1)

            def x_outputs(half):
                pe.wait_ge(sx_pT, 4 * half + 4)
                for j in range(KT):
                    g = G_PV + half * KT + j
                    pe.wait_ge(tile_out, g - 1)
                    h = j // 2
                    for c in range(MT):
                        mm = nc.tensor.matmul(psG[g % 2][:], vx[:, c, j * P:(j + 1) * P], pTx[:, 2 * h + c, :],
                                              start=(c == 0), stop=(c == MT - 1))
                    mm.then_inc(tile_done, 1)

            pe.wait_ge(tile_out, G_PV)
            x_scores(0)
            x_scores(1)
            for t in range(TT):
                x_transposes(t)
                if t + 2 < TT:
                    x_scores(t + 2)
                if t % 4 == 3:
                    x_outputs(t // 4)

            def before_xo(half, t):
                if half == 0 and t == 0:
                    pe.wait_ge(tile_out, G_PV + 2 * KT)
            residual_product(G_XO, C_XO, XO_SLOTS, N_X, x_hn, before_xo)

            def mlp_group(g):
                for j in range(8):
                    half, c = divmod(j, 4)
                    first = isinstance(g, int)
                    if half == 0:
                        pe.wait_ge(lo_done, g * 8 + (B_BLOCKS + C_MLP + c + 1))
                    if first and c == 0:
                        pe.wait_ge(n_lo, N_X + (half + 1) * TT // 2)
                    pe.wait_ge(tile_out, g * MLP_TILES + (G_MLP + j - 1))
                    tok = slice(half * HALF, (half + 1) * HALF)
                    split_products(psG[j % 2][:], [(*col_block(w_hi[MLP_SLOTS[c]], w_lo[MLP_SLOTS[c]], k), act_hi[:, k, tok], act_lo[:, k, tok])
                                                   for k in range(KT)]).then_inc(tile_done, 1)
                    if first and j == 1:
                        last_norm_trs(N_X, x_hn)
                for t in range(TT):
                    for half in range(2):
                        j = 8 + 2 * t + half
                        cs = slice(half * HALF, (half + 1) * HALF)
                        if t == 0 and half == 0:
                            pe.wait_ge(lo_done, g * 8 + (B_BLOCKS + C_MLP + 8))
                        pe.wait_ge(tile_out, g * MLP_TILES + (G_MLP + j - 1))
                        tok = slice(t * P, (t + 1) * P)
                        split_products(psG[half][:], [(a_hi[:, c, tok], a_lo[:, c, tok], w_hi[MLP_SLOTS[4 + c]][:, cs], w_lo[MLP_SLOTS[4 + c]][:, cs])
                                                      for c in range(4)]).then_inc(tile_done, 1)

            mlp_group(0)
            with pe.Fori(1, GROUPS) as g:
                mlp_group(g)

        @block.scalar
        def _(act):
            def split_hi(dst, src, sem_, *waits):
                for s_, v in waits:
                    act.wait_ge(s_, v)
                nc.scalar.activation(dst, src, ACT.Copy).then_inc(sem_, 1)

            def sq(n, src, *waits):
                for s_, v in waits:
                    act.wait_ge(s_, v)
                if n:
                    act.wait_ge(n_sq, n)
                nc.scalar.activation(psO[:].rearrange("p a n -> p (a n)"), src, ACT.Square, accum_out=sum_sq[:, n % 2:n % 2 + 1]).then_inc(n_sq, 1)

            def root(n):
                i = slice(n % 2, n % 2 + 1)
                act.wait_ge(n_var, n + 1)
                nc.scalar.activation(std[:, i], var[:, i], ACT.Sqrt).then_inc(n_std, 1)

            def norm_hi(n, dst):
                act.wait_ge(n_tr, n + 1)
                nc.scalar.activation(dst, psS[n % 2][:].rearrange("p (k t) -> p k t", t=P), ACT.Copy).then_inc(n_hi, 1)

            def act_tile(t):
                return act_hi[:, :, t * P:(t + 1) * P]

            for t in range(TT + 2):
                if t < TT:
                    sq(t, X[:, t, :], (x_loaded[t], 16))
                if 1 <= t <= TT:
                    root(t - 1)
                if t >= 2:
                    norm_hi(t - 2, act_tile(t - 2))
                if t in (4, 5, 6):
                    split_hi((w_hi[0], w_hi[1], first_k[0])[t - 4][:], raw[0][:], hi_done, (rawB, 16 * (t - 3)))
            split_hi(gate_hi[:], gate_raw[:], gate_hi_done, (gate_loaded, 16))

            def qk_hi_out(j, chunk, half, a):
                tok = slice(half * HALF, (half + 1) * HALF)
                for h in range(2):
                    src = psG[j % 2][h * HEAD:(h + 1) * HEAD, :]
                    places = (qhl[a][h][0:HEAD, tok], qb_[a][h][0:HEAD, tok]) if chunk == Q_ else \
                             (khh[a][h][0:HEAD, tok], khh[a][h][HEAD:P, tok])
                    for dst in places:
                        e = nc.scalar.activation(dst, src, ACT.Copy, scale=1.0 / math.sqrt(HEAD) if chunk == Q_ else 1.0)
                e.then_inc(qk_hi, 1)

            for j, (chunk, half) in enumerate(FIRST_TILES):
                if chunk in (Q_, K_) and j < PRO_TILES - 1:
                    act.wait_ge(tile_done, j + 1)
                    qk_hi_out(j, chunk, half, 0)
                if chunk == V_ and half == 1:
                    act.wait_ge(tile_out, 5)
                    nc.scalar.activation(gate_e[:], gate_z[:], ACT.Abs).then_inc(gate_act, 1)
                    act.wait_ge(gate_act, 1)
                    nc.scalar.activation(gate_e[:], gate_e[:], ACT.Exp, scale=-1.0).then_inc(gate_act, 1)
                    act.wait_ge(gate_act, 2)
                    nc.scalar.activation(gate_e[:], gate_e[:], ACT.Ln, bias=1.0).then_inc(gate_act, 1)
                if chunk == Q_ and half == 1:
                    split_hi(w_hi[1][:], raw[0][:], hi_done, (rawB, 64))

            def exp_step(u, value):
                n = (u % QB + 1) * P
                act.wait_ge(max_done, value)
                nc.scalar.activation(S[:, 0:n], S[:, 0:n], ACT.Exp, bias=row_max[:, u % 2:u % 2 + 1], scale=-1.0,
                                     accum_out=row_sum[:, u % 2:u % 2 + 1]).then_inc(exp_done, 1)

            exp_step(0, 1)

            act.wait_ge(cum_stored, 64)

            def block_hi(m, slot, value=None, i=None):
                if m is not None:
                    i, n = raw_of(m)
                    value = 16 * n
                act.wait_ge(rawC[i], value)
                nc.scalar.activation(w_hi[slot][:], raw[i][:], ACT.Copy).then_inc(hi_done, 1)

            def pair_act(p, par, has_next, splits):
                for ev in pair_steps(has_next):
                    kind, u = ev[0], ev[1]
                    if kind == "T":
                        n = (u % QB + 1) * P
                        act.wait_ge(tr_done, p * 16 + (u + 1))
                        nc.scalar.activation(pT[:, 0:n], psS[u % 2][:, 0:n], ACT.Copy).then_inc(pT_done, 1)
                        if not has_next and u in OUT_STEPS:
                            m = OUT_STEPS.index(u)
                            block_hi(C_OUT + m, OUT_SLOTS[m])
                    elif kind == "QK":
                        exp_step(u, p * 16 + (u + 1))
                    elif kind == "last":
                        act.wait_ge(tile_done, body_tile(p, -1))
                        qk_hi_out(LAST, *PAIR_TILES[LAST], par)
                    elif kind == "tile" and PAIR_TILES[u][0] != V_ and u != LAST:
                        act.wait_ge(tile_done, body_tile(p, u))
                        qk_hi_out(u, *PAIR_TILES[u], 1 - par)
                    ahead = SPLIT_AT.get((kind, u))
                    if ahead and has_next and (splits or ahead < 3):
                        act.wait_ge(tile_done, body_tile(p, {1: -1, 2: 1, 3: 4}[ahead]))
                        split_hi(w_hi[pair_slot(par, ahead)][:], raw[0][:], hi_done, (rawB, p * 48 + 16 * (3 + ahead + 1)))

            with act.Fori(0, 3) as it:
                for par in range(2):
                    pair_act(it * 2 + par, par, True, True)
            pair_act(6, 0, True, False)
            pair_act(7, 1, False, False)
            for t in range(TT):
                act.wait_ge(yt_done, t + 1)
                nc.scalar.activation(act_tile(t), psS[t % 2][:].rearrange("p (k t) -> p k t", t=P), ACT.Copy).then_inc(y_hi, 1)
                if t in (1, 2, 3, 4):
                    block_hi(C_OUT + 3 + t, OUT_SLOTS[3 + t])

            for t in range(MT):
                n = N_M + t
                sq(n, m_in[:], (m_loaded[t], 16))
                root(n)
            for t in range(MT):
                norm_hi(N_M + t, mT_hi[:, :, t * P:(t + 1) * P])

            def residual_norm_act(g0, n0, extra):
                for t in range(TT):
                    n = n0 + t
                    sq(n, X[:, t, :], (tile_out, g0 + TT + t + 1))
                    root(n)
                    if t >= 2:
                        norm_hi(n - 2, act_tile(t - 2))
                    extra(t)

            def last_norm_his(n0):
                for t in (TT - 2, TT - 1):
                    norm_hi(n0 + t, act_tile(t))

            def extra_c(t):
                if t in (2, 3):
                    block_hi(C_XK + t - 2, X_SLOTS[t - 2])

            residual_norm_act(G_OUT, N_C, extra_c)
            with act.Fori(0, 4) as c:
                for i in range(2):
                    act.wait_ge(tile_done, c * 2 + (G_XK + i + 1))
                    block_hi(None, X_SLOTS[i], c * 16 + 16 * raw_of(C_XK + 2 + i)[1], i)
            last_norm_his(N_C)
            with act.Fori(0, 4) as c:
                for i in range(2):
                    act.wait_ge(tile_done, c * 4 + (G_XV + 2 * i + 1))
                    block_hi(None, X_SLOTS[i], c * 16 + 16 * raw_of(C_XV + 2 + i)[1], i)
            with act.Fori(0, 4) as c:
                for i in range(2):
                    act.wait_ge(tile_done, c * 4 + (G_XQ + 2 * i + 2))
                    block_hi(None, X_SLOTS[i], c * 16 + 16 * raw_of(C_XQ + 2 + i)[1], i)
            block_hi(C_XO + 2, XO_SLOTS[2])

            def x_exp(t):
                act.wait_ge(sx_neg, t + 1)
                for h in range(X_HEADS):
                    e = nc.scalar.activation(Sx[t % 2][:, h, :], psS[t % 2][:, h * N_MEM:(h + 1) * N_MEM], ACT.Exp,
                                             bias=x_neg[:, t % 2, h:h + 1], accum_out=x_sum[:, t % 2, h:h + 1])
                e.then_inc(sx_exp, 1)

            def x_pT(t):
                if t == 4:
                    act.wait_ge(tile_done, G_PV + KT)
                act.wait_ge(sx_tr, t + 1)
                o = (t % 4) * P
                nc.scalar.activation(pTx[:, :, o:o + P], psS[t % 2][:].rearrange("p (b t) -> p b t", t=P), ACT.Copy).then_inc(sx_pT, 1)

            def x_out(half):
                for j in range(KT):
                    g = G_PV + half * KT + j
                    act.wait_ge(tile_done, g + 1)
                    nc.scalar.activation(act_hi[:, j, half * HALF:(half + 1) * HALF], psG[g % 2][:], ACT.Copy).then_inc(hi_out, 1)

            x_exp(0)
            x_exp(1)
            for t in range(TT):
                x_pT(t)
                if t % 4 == 3:
                    if t + 2 < TT:
                        x_exp(t + 2)
                    x_out(t // 4)
                elif t + 2 < TT:
                    x_exp(t + 2)
            for m in range(3, 8):
                if m == 3:
                    act.wait_ge(tile_done, G_XO)
                block_hi(C_XO + m, XO_SLOTS[m])

            def extra_x(t):
                if t in (2, 3, 4, 5):
                    block_hi(C_MLP + t - 2, MLP_SLOTS[t - 2])
            residual_norm_act(G_XO, N_X, extra_x)
            def mlp_group(g, first, last):
                for j in range(8):
                    half, c = divmod(j, 4)
                    act.wait_ge(tile_done, g * MLP_TILES + (G_MLP + j + 1))
                    act.wait_ge(tile_out, g * MLP_TILES + (G_MLP + j - 1))
                    nc.scalar.activation(r_ff[:, j % 2, :], psG[j % 2][:], ACT.Relu).then_inc(relu_out, 1)
                    act.wait_ge(sq_out, g * 8 + (j + 1))
                    nc.scalar.activation(a_hi[:, c, half * HALF:(half + 1) * HALF], r_ff[:, j % 2, :], ACT.Copy).then_inc(hi_out, 1)
                    if first and j == 1:
                        last_norm_his(N_X)
                    if first and 2 <= j < 6:
                        block_hi(C_MLP + 2 + j, MLP_SLOTS[2 + j])
                    if half == 1 and not last and not first:
                        block_hi(None, MLP_SLOTS[c], g * 64 + 16 * raw_of(C_MLP + 8 + c)[1], c % 2)
                if not last:
                    if first:
                        for c in range(4):
                            block_hi(C_MLP + 8 + c, MLP_SLOTS[c])
                    act.wait_ge(tile_done, g * MLP_TILES + (G_MLP + MLP_TILES))
                    for c in range(4, 8):
                        block_hi(None, MLP_SLOTS[c], g * 64 + 16 * raw_of(C_MLP + 8 + c)[1], c % 2)

            mlp_group(0, True, False)
            with act.Fori(1, GROUPS - 1) as g:
                mlp_group(g, False, False)
            mlp_group(GROUPS - 1, False, True)
            for t in range(TT):
                n = N_F + t
                sq(n, X[:, t, :], (tile_out, G_MLP + (GROUPS - 1) * MLP_TILES + 8 + 2 * t + 2))
                root(n)

        @block.vector
        def _(dve):
            def lo_part(dst, src, hi, sem_):
                nc.vector.tensor_tensor(dst, src, hi.bitcast(f32), ALU.subtract).then_inc(sem_, 1)

            def norm_var(n):
                i = slice(n % 2, n % 2 + 1)
                dve.wait_ge(n_sq, n + 1)
                nc.vector.tensor_scalar(var[:, i], sum_sq[:, i], 1.0 / D, EPS, ALU.mult, ALU.add).then_inc(n_var, 1)

            def norm_scale(n, src, dst, gain_t, *waits):
                i = slice(n % 2, n % 2 + 1)
                dve.wait_ge(n_std, n + 1)
                nc.vector.reciprocal(rstd0[:, i], std[:, i]).then_inc(n_chain, 1)
                dve.wait_ge(n_chain, 4 * n + 1)
                nc.vector.scalar_tensor_tensor(newt[:, 0, i], rstd0[:, i], rstd0[:, i], var[:, i], ALU.mult, ALU.mult).then_inc(n_chain, 1)
                dve.wait_ge(n_chain, 4 * n + 2)
                nc.vector.tensor_scalar(newt[:, 1, i], newt[:, 0, i], -0.5, 1.5, ALU.mult, ALU.add).then_inc(n_chain, 1)
                dve.wait_ge(n_chain, 4 * n + 3)
                nc.vector.tensor_tensor(rstd[:, i], rstd0[:, i], newt[:, 1, i], ALU.mult).then_inc(n_chain, 1)
                dve.wait_ge(n_chain, 4 * n + 4)
                for s_, v in waits:
                    dve.wait_ge(s_, v)
                nc.vector.scalar_tensor_tensor(dst[:], src, rstd[:, i], gain_t[:], ALU.mult, ALU.mult).then_inc(n_hn, 1)

            def norm_lo(n, dst_lo, dst_hi):
                dve.wait_ge(n_hi, n + 1)
                lo_part(dst_lo, psS[n % 2][:].rearrange("p (k t) -> p k t", t=P), dst_hi, n_lo)

            def act_tile(a, t):
                return a[:, :, t * P:(t + 1) * P]

            def block_lo(n, slot, raw_slot, places=None):
                dve.wait_ge(hi_done, n + 1)
                hi, lo = places or (w_hi[slot], w_lo[slot])
                lo_part(lo[:], raw[raw_slot][:], hi[:], lo_done)

            def later_lo(m, slot):
                block_lo(B_BLOCKS + m, slot, raw_of(m)[0])

            nc.vector.memset(gate_raw[:], 0.0).then_inc(gate_zeroed, 1)
            for t in range(TT + 2):
                if t < TT:
                    norm_var(t)
                if 1 <= t <= TT:
                    if t >= 3:
                        dve.wait_ge(n_tr, t - 2)
                    norm_scale(t - 1, X[:, t - 1, :], a_hn[(t - 1) % 2], a_gain, (gain_loaded[0], 16))
                if t >= 2:
                    norm_lo(t - 2, act_tile(act_lo, t - 2), act_tile(act_hi, t - 2))
                if t in (4, 5, 6):
                    block_lo(t - 4, t - 4, 0, first_k if t == 6 else None)
            dve.wait_ge(gate_hi_done, 1)
            lo_part(gate_lo[:], gate_raw[:], gate_hi[:], gate_lo_done)

            def tile_rest(j, chunk, half, a, hi_count):
                tok = slice(half * HALF, (half + 1) * HALF)
                if chunk == V_:
                    nc.vector.tensor_copy(vT[:, tok], psG[j % 2][:]).then_inc(tile_out, 1)
                else:
                    dve.wait_ge(qk_hi, hi_count)
                    for h in range(2):
                        src = psG[j % 2][h * HEAD:(h + 1) * HEAD, :]
                        if chunk == Q_:
                            e = nc.vector.scalar_tensor_tensor(qhl[a][h][HEAD:P, tok], src, 1.0 / math.sqrt(HEAD),
                                                               qhl[a][h][0:HEAD, tok].bitcast(f32), ALU.mult, ALU.subtract)
                        else:
                            e = nc.vector.tensor_tensor(klb[a][h][0:HEAD, tok], src, khh[a][h][0:HEAD, tok].bitcast(f32),
                                                        ALU.subtract)
                    e.then_inc(tile_out, 1)

            def v_out(i, a):
                nc.vector.tensor_copy(V[a][:, 4 * i:4 * i + 4, :],
                                      psS[i][:, HALF:2 * HALF].rearrange("p (b d) -> p b d", d=P)).then_inc(vt_out, 1)

            dve.wait_ge(b_loaded, 16)
            for j, (chunk, half) in enumerate(FIRST_TILES):
                if j == PRO_TILES - 1:
                    break
                dve.wait_ge(tile_done, j + 1)
                if chunk == GATE_:
                    nc.vector.tensor_scalar(gate_z[:, half * HALF:(half + 1) * HALF], psG[j % 2][0:8, :], b_col[:], None,
                                            ALU.add).then_inc(tile_out, 1)
                else:
                    tile_rest(j, chunk, half, 0, {1: 1, 2: 2, 6: 3, 7: 4}.get(j))
                if j == 6:
                    block_lo(3, 1, 0)
                if j == 5:
                    dve.wait_ge(gate_act, 1)
                    nc.vector.tensor_scalar(gate_z[:], gate_z[:], -1.0, 0.0, ALU.mult, ALU.max).then_inc(gate_dve, 1)
                    dve.wait_ge(gate_dve, 1)
                    dve.wait_ge(gate_act, 3)
                    nc.vector.tensor_tensor(gate_z[:], gate_z[:], gate_e[:], ALU.add).then_inc(gate_dve, 1)
                    dve.wait_ge(gate_dve, 2)
                    nc.vector.tensor_tensor_scan(cum[:], gate_z[:], gate_z[:], 0.0, ALU.add, ALU.bypass).then_inc(gate_dve, 1)
                    dve.wait_ge(gate_dve, 3)
                    nc.vector.tensor_copy(cum_hi[:], cum[:]).then_inc(gate_dve, 1)
                    dve.wait_ge(gate_dve, 4)
                    nc.vector.tensor_tensor(cum_lo[:], cum[:], cum_hi[:].bitcast(f32), ALU.subtract).then_inc(gate_dve, 1)
                    dve.wait_ge(gate_dve, 5)
                    nc.vector.tensor_scalar(gate_z[:], cum_hi[:].bitcast(f32), -1.0, None, ALU.mult).then_inc(gate_dve, 1)
                    nc.vector.tensor_scalar(gate_e[:], cum_lo[:].bitcast(f32), -1.0, None, ALU.mult).then_inc(gate_dve, 1)

            def max_step(u, value):
                n = (u % QB + 1) * P
                dve.wait_ge(qk_done, value)
                dve.sem_inc(max_gate, 1)
                nc.vector.tensor_tensor_reduce(out=S[:, 0:n], in0=psS[u % 2][:, 0:n], in1=mask[:, T - n:T], scale=-1.0,
                                               scalar=3.0e38, op0=ALU.add, op1=ALU.min,
                                               accum_out=row_max[:, u % 2:u % 2 + 1]).then_inc(max_done, 1)

            for i in range(2):
                dve.wait_ge(vt_done, i + 1)
                v_out(i, 0)
            dve.wait_ge(mask_loaded, 16)
            max_step(0, 1)
            dve.wait_ge(cum_stored, 64)

            def pair_dve(it, p, par, has_next, splits):
                for ev in pair_steps(has_next):
                    kind, u = ev[0], ev[1]
                    h, qb = divmod(u % STEPS, QB)
                    if kind == "QK":
                        if u == STEPS and splits and par == 1:
                            dve.wait_ge(mask_loaded, it * 16 + 32)
                        max_step(u, p * 16 + (u + 1))
                    elif kind == "PV":
                        i = slice(u % 2, u % 2 + 1)
                        dve.wait_ge(exp_done, p * 16 + (u + 1))
                        nc.vector.reciprocal(row_inv[:, i], row_sum[:, i]).then_inc(inv_done, 1)
                        dve.wait_ge(inv_done, p * 16 + (u + 1))
                        dve.wait_ge(pv_done, p * 16 + (u + 1))
                        dst = X[:, qb, bass.ds(p * P + h * HEAD, HEAD)]
                        nc.vector.tensor_scalar(dst, psO[:, u % 2, 0:HEAD], row_inv[:, i], None,
                                                ALU.mult).then_inc(o_out, 1)
                    elif kind == "tile":
                        chunk, half = PAIR_TILES[u]
                        dve.wait_ge(tile_done, body_tile(p, u))
                        if u != LAST:
                            tile_rest(u, chunk, half, 1 - par, p * 4 + (4 + QK_COUNT.get(u, 0)))
                    elif kind == "last":
                        dve.wait_ge(tile_done, body_tile(p, -1))
                        tile_rest(LAST, *PAIR_TILES[LAST], par, p * 4 + 4)
                    elif kind == "VT":
                        dve.wait_ge(vt_done, p * 2 + (u + 3))
                        v_out(u, 1 - par)
                    elif kind == "T" and not has_next and u in OUT_STEPS:
                        m = OUT_STEPS.index(u)
                        later_lo(C_OUT + m, OUT_SLOTS[m])
                    ahead = SPLIT_AT.get((kind, u))
                    if ahead and has_next and (splits or ahead < 3):
                        block_lo(p * 3 + (3 + ahead), pair_slot(par, ahead), 0)

            with dve.Fori(0, 3) as it:
                for par in range(2):
                    pair_dve(it, it * 2 + par, par, True, True)
            pair_dve(3, 6, 0, True, False)
            pair_dve(3, 7, 1, False, False)

            def y_split(t):
                dve.wait_ge(y_hi, t + 1)
                lo_part(act_tile(act_lo, t), psS[t % 2][:].rearrange("p (k t) -> p k t", t=P), act_tile(act_hi, t), y_lo)

            def add_residual(g, t, half):
                dve.wait_ge(tile_done, g + 1)
                cs = slice(half * HALF, (half + 1) * HALF)
                nc.vector.tensor_tensor(X[:, t, cs], X[:, t, cs], psG[g % 2][:], ALU.add).then_inc(tile_out, 1)

            for t in range(TT):
                y_split(t)
                if t in (1, 2, 3, 4):
                    later_lo(C_OUT + 3 + t, OUT_SLOTS[3 + t])
                if t >= 1:
                    dve.wait_ge(x_loaded[t - 1], 32)
                    add_residual(G_OUT + t - 1, t - 1, 0)
            dve.wait_ge(x_loaded[TT - 1], 32)
            add_residual(G_OUT + TT - 1, TT - 1, 0)

            for t in range(MT):
                n = N_M + t
                norm_var(n)
                norm_scale(n, m_in[:], c_hn[n % 2], m_gain, (gain_loaded[2], 16))
            for t in range(MT):
                norm_lo(N_M + t, mT_lo[:, :, t * P:(t + 1) * P], mT_hi[:, :, t * P:(t + 1) * P])

            def residual_norm_dve(g0, n0, hn, gain_t, gain_sem, extra):
                for t in range(TT):
                    n = n0 + t
                    add_residual(g0 + TT + t, t, 1)
                    norm_var(n)
                    if t >= 2:
                        norm_lo(n - 2, act_tile(act_lo, t - 2), act_tile(act_hi, t - 2))
                    norm_scale(n, X[:, t, :], hn[n % 2], gain_t, (gain_sem, 16), (n_tr, n - 1))
                    extra(t)

            def last_norm_los(n0):
                for t in (TT - 2, TT - 1):
                    norm_lo(n0 + t, act_tile(act_lo, t), act_tile(act_hi, t))

            def extra_c(t):
                if t in (2, 3):
                    later_lo(C_XK + t - 2, X_SLOTS[t - 2])
            residual_norm_dve(G_OUT, N_C, c_hn, c_gain, gain_loaded[1], extra_c)

            with dve.Fori(0, 4) as c:
                for i in range(2):
                    dve.wait_ge(tile_done, c * 2 + (G_XK + i + 1))
                    nc.vector.tensor_copy(kx[:, bass.ds(c * 2 + i, 1), :].rearrange("p o n -> p (o n)"),
                                          psG[(G_XK + i) % 2][:, 0:N_MEM]).then_inc(tile_out, 1)
                    block_lo(c * 2 + (B_BLOCKS + C_XK + 2 + i), X_SLOTS[i], i)
            last_norm_los(N_C)
            with dve.Fori(0, 4) as c:
                for i in range(2):
                    dve.wait_ge(tile_done, c * 4 + (G_XV + 2 * i + 1))
                    nc.vector.tensor_copy(vxT[:, i, :], psG[0][:, 0:N_MEM]).then_inc(tile_out, 1)
                    dve.wait_ge(tile_done, c * 4 + (G_XV + 2 * i + 2))
                    nc.vector.tensor_copy(vx[:, :, bass.ds(c * 256 + i * P, P)],
                                          psG[1][:, 0:N_MEM].rearrange("p (b d) -> p b d", d=P)).then_inc(tile_out, 1)
                    block_lo(c * 2 + (B_BLOCKS + C_XV + 2 + i), X_SLOTS[i], i)
            with dve.Fori(0, 4) as c:
                for i in range(2):
                    for half in range(2):
                        dve.wait_ge(tile_done, c * 4 + (G_XQ + 2 * i + half + 1))
                        nc.vector.tensor_scalar(qx[:, bass.ds(c * 2 + i, 1), half * HALF:(half + 1) * HALF].rearrange("p o n -> p (o n)"),
                                                psG[half][:], 1.0 / math.sqrt(D // X_HEADS), None, ALU.mult).then_inc(tile_out, 1)
                    block_lo(c * 2 + (B_BLOCKS + C_XQ + 2 + i), X_SLOTS[i], i)
            later_lo(C_XO + 2, XO_SLOTS[2])

            def x_row_max(t):
                dve.wait_ge(sx_done, t + 1)
                nc.vector.tensor_reduce(x_max[:, t % 2, :], psS[t % 2][:].rearrange("p (h n) -> p h n", n=N_MEM),
                                        AX.X, ALU.max).then_inc(sx_max, 1)
                dve.wait_ge(sx_max, t + 1)
                nc.vector.tensor_scalar(x_neg[:, t % 2, :], x_max[:, t % 2, :], -1.0, None, ALU.mult).then_inc(sx_neg, 1)

            def x_normalise(t):
                dve.wait_ge(sx_exp, t + 1)
                nc.vector.reciprocal(x_inv[:, t % 2, :], x_sum[:, t % 2, :]).then_inc(sx_inv, 1)
                dve.wait_ge(sx_inv, t + 1)
                nc.vector.tensor_tensor(Sx[t % 2][:], Sx[t % 2][:],
                                        x_inv[:, t % 2, :].rearrange("p (h o) -> p h o", o=1).to_broadcast([P, X_HEADS, N_MEM]),
                                        ALU.mult).then_inc(sx_norm, 1)

            def x_out_lo(half):
                for j in range(KT):
                    g = G_PV + half * KT + j
                    dve.wait_ge(hi_out, half * KT + j + 1)
                    cs = slice(half * HALF, (half + 1) * HALF)
                    lo_part(act_lo[:, j, cs], psG[g % 2][:], act_hi[:, j, cs], tile_out)

            x_row_max(0)
            x_row_max(1)
            for t in range(TT):
                x_normalise(t)
                if t + 2 < TT:
                    x_row_max(t + 2)
                if t % 4 == 3:
                    x_out_lo(t // 4)
            for m in range(3, 8):
                later_lo(C_XO + m, XO_SLOTS[m])
            for t in range(TT):
                add_residual(G_XO + t, t, 0)

            def extra_x(t):
                if t in (2, 3, 4, 5):
                    later_lo(C_MLP + t - 2, MLP_SLOTS[t - 2])
            residual_norm_dve(G_XO, N_X, x_hn, x_gain, gain_loaded[3], extra_x)

            def mlp_group(g, first, last):
                for j in range(8):
                    half, c = divmod(j, 4)
                    cs = slice(half * HALF, (half + 1) * HALF)
                    dve.wait_ge(relu_out, g * 8 + (j + 1))
                    nc.vector.tensor_tensor(r_ff[:, j % 2, :], r_ff[:, j % 2, :], r_ff[:, j % 2, :], ALU.mult).then_inc(sq_out, 1)
                    dve.wait_ge(hi_out, g * 8 + (2 * KT + j + 1))
                    lo_part(a_lo[:, c, cs], r_ff[:, j % 2, :], a_hi[:, c, cs], tile_out)
                    if first and j == 1:
                        last_norm_los(N_X)
                    if first and 2 <= j < 6:
                        later_lo(C_MLP + 2 + j, MLP_SLOTS[2 + j])
                    if half == 1 and not last and not first:
                        block_lo(g * 8 + (B_BLOCKS + C_MLP + 8 + c), MLP_SLOTS[c], c % 2)
                if first:
                    for c in range(4):
                        later_lo(C_MLP + 8 + c, MLP_SLOTS[c])
                for t in range(TT):
                    for half in range(2):
                        dve.wait_ge(tile_done, g * MLP_TILES + (G_MLP + 8 + 2 * t + half + 1))
                        cs = slice(half * HALF, (half + 1) * HALF)
                        nc.vector.tensor_tensor(X[:, t, cs], X[:, t, cs], psG[half][:], ALU.add).then_inc(tile_out, 1)
                    if last:
                        final_norm(t)
                if not last:
                    for c in range(4, 8):
                        block_lo(g * 8 + (B_BLOCKS + C_MLP + 8 + c), MLP_SLOTS[c], c % 2)

            def final_norm(t):
                norm_var(N_F + t)
                if t:
                    final_scale(t - 1)

            def final_scale(t):
                n = N_F + t
                if t >= 2:
                    dve.wait_ge(out_stored[n % 2], 16 * (t // 2))
                norm_scale(n, X[:, t, :], f_hn[n % 2], f_gain, (gain_loaded[4], 16))

            mlp_group(0, True, False)
            with dve.Fori(1, GROUPS - 1) as g:
                mlp_group(g, False, False)
            mlp_group(GROUPS - 1, False, True)
            final_scale(TT - 1)


_INS = ["x", "mem", "g_mix", "w_in", "b_forget", "w_out", "g_xattn", "g_mem", "w_xq", "w_xk", "w_xv", "w_xo",
        "g_mlp", "w_up", "w_down", "g_final"]


def _shape_constants():
    ident = np.eye(P, dtype=np.float32)
    delta = (T - P) + np.arange(P)[:, None] - np.arange(T)[None, :]
    times = sum(((delta >= 0) & (delta <= w) & (delta % d == 0)).astype(np.int64) for w, d in DILATIONS)
    dilated = np.where(times > 0, np.log(np.maximum(times, 1)), NEG).astype(np.float32)
    causal = np.where(delta >= 0, 0.0, NEG).astype(np.float32)
    slopes = 2.0 ** -np.arange(1, 9, dtype=np.float64)
    bias = np.zeros((2 * PAIRS, 8, T), np.float32)
    bias[:, (0, 1, 6, 7), :] = 1.0
    alibi = (slopes[:, None] * np.arange(T)[None, :]).astype(np.float32)
    bias[:PAIRS, 2], bias[:PAIRS, 4] = -alibi, alibi
    return {"ident": ident, "masks": np.stack([dilated, dilated, causal, causal]), "bias": bias}


def kernel(**inputs):
    import concourse.bacc as _bacc
    from concourse.bass_utils import run_bass_kernel_spmd as _run

    nc = _bacc.Bacc("TRN2", target_bir_lowering=False, num_devices=1)
    arrays, args = {}, []
    for name in _INS:
        a = np.ascontiguousarray(inputs[name])
        arrays[f"in_{name}_dram"] = a
        args.append(nc.dram_tensor(f"in_{name}_dram", a.shape, mybir.dt.from_np(a.dtype), kind="ExternalInput").ap())
    for name, a in _shape_constants().items():
        arrays[f"const_{name}_dram"] = a
        args.append(nc.dram_tensor(f"const_{name}_dram", a.shape, mybir.dt.from_np(a.dtype), kind="ExternalInput").ap())
    args.append(nc.dram_tensor("out_0_dram", (1, T, D), mybir.dt.float32, kind="ExternalOutput").ap())
    hybrid_layer(nc, *args)
    r = _run(nc, [arrays], core_ids=[0])
    return r.results[0]["out_0_dram"]
```

```python
import math
from contextlib import ExitStack

import numpy as np

import concourse.bass as bass
from concourse import mybir

P = 128
T = 1024
D = 1024
KT = D // P
TT = T // P
HALF = 512
N_MEM = 256
MT = N_MEM // P
HEAD = 64
PAIRS = 8
STEPS = 16
X_HEADS = 4
D_FF = 4096
GROUPS = D_FF // HALF
EPS = 1e-6
NEG = -1e30
DILATIONS = ((128, 1), (512, 4), (2048, 16))
GATE_COL = 6 * PAIRS // 2 * P
KB = 1024


V_, Q_, K_, GATE_ = range(4)
PAIR_TILES = ((V_, 0), (V_, 1), (Q_, 0), (K_, 0), (Q_, 1), (K_, 1))
FIRST_TILES = ((V_, 0), (Q_, 0), (K_, 0), (GATE_, 0), (GATE_, 1), (V_, 1), (Q_, 1), (K_, 1))
PRODUCTS = 3 * KT


KEY_BLOCKS = (1, 2, 3, 8, 1, 8, 2, 7, 4, 7, 3, 6, 4, 6, 5, 5)
STEP = tuple((KEY_BLOCKS[:u].count(n), n - 1) for u, n in enumerate(KEY_BLOCKS))
S_BLOCKS = 11


def gaps():
    room = []
    for u in range(STEPS):
        n, n1 = KEY_BLOCKS[u], KEY_BLOCKS[(u + 1) % STEPS]
        first = 1.0 + 0.15 * n
        room += [first, max(0.2, 2.3 + 0.18 * n1 - 0.07 * n - first)]
    return room


def pair_steps(has_next):
    room = gaps()
    total = PRODUCTS * len(PAIR_TILES) if has_next else 0
    order = []
    done = early = 0
    complete = None
    for u in range(STEPS):
        if u + 1 < STEPS or has_next:
            order.append(("QK", u + 1))
        order.append(("T", u))
        if u in VT_STEPS and has_next:
            order.append(("VT", VT_STEPS.index(u)))
        if u == 0:
            order.append(("last", len(PAIR_TILES) - 1))
        if complete is not None:
            order.append(("tile", complete))
            complete = None
        for part in range(2):
            upto = round(total * sum(room[:2 * u + part + 1]) / sum(room))
            while done < upto:
                j, r0 = divmod(done, PRODUCTS)
                r1 = min(PRODUCTS, r0 + upto - done)
                order.append(("G", j, r0, r1))
                if r1 == PRODUCTS:
                    complete = j
                done += r1 - r0
            if not has_next:
                if u in Y_STEPS:
                    order.append(("Y", 2 * Y_STEPS.index(u) + part))
                elif u > Y_STEPS[-1] and part == 0:
                    upto = round(EARLY_PRODUCTS * (u - Y_STEPS[-1]) / (STEPS - 1 - Y_STEPS[-1]))
                    while early < upto:
                        t, r0 = divmod(early, Y_PRODUCTS)
                        r1 = min(Y_PRODUCTS, r0 + upto - early)
                        order.append(("P", t, r0, r1))
                        early += r1 - r0
            if part == 0:
                order.append(("PV", u))
    return order


X_STEPS = [("S", 0), ("S", 1), ("N", 0), ("S", 2), ("N", 1), ("Q",), ("N", 2),
           ("T", 0), ("T", 1), ("S", 3), ("S", 4), ("N", 3),
           ("T", 2), ("O", 0, 0), ("N", 4), ("S", 5),
           ("T", 3), ("O", 0, 1), ("N", 5), ("S", 6),
           ("T", 4), ("O", 1, 0), ("N", 6), ("S", 7),
           ("T", 5), ("O", 1, 1), ("N", 7),
           ("T", 6), ("O", 2, 0), ("T", 7), ("O", 2, 1), ("O", 3, 0), ("O", 3, 1)]
Q_LAST = ((0, 0), (1, 0), (0, 1), (1, 1))

Y_STEPS = (1, 2, 3, 4, 5, 6, 7, 8)
Y_PRODUCTS = 3 * (PAIRS - 1)
EARLY_PRODUCTS = 2 * Y_PRODUCTS - 4
VT_STEPS = (8, 10)


def hybrid_layer(nc, x, mem, g_mix, w_in, b_forget, w_out, g_xattn, g_mem, w_xq, w_xk, w_xv, w_xo,
                 g_mlp, w_up, w_down, g_final, ident_c, masks_c, bias_c, out):
    f32, f32r = mybir.dt.float32, mybir.dt.float32r
    ALU, ACT, AX = mybir.AluOpType, mybir.ActivationFunctionType, mybir.AxisListType

    x_t = x[0].rearrange("(t p) d -> t p d", p=P)
    out_t = out[0].rearrange("(t p) d -> t p d", p=P)
    mem_t = mem[0].rearrange("(t p) d -> t p d", p=P)

    def k_rows(w):
        return w.rearrange("(k p) n -> p k n", p=P)

    w_in_k, w_out_k, w_xq_k, w_xk_k, w_xv_k, w_xo_k, w_up_k = map(
        k_rows, (w_in, w_out, w_xq, w_xk, w_xv, w_xo, w_up))
    bias_rows = nc.dram_tensor("bias_rows", (2 * PAIRS, 8, T), f32).ap()

    base = 16 * KB + 448

    def at(name, shape, dt, kb):
        return nc.alloc_sbuf_tensor_at(name, shape, dt, offset=base + int(kb * KB))

    act_hi = at("act_hi", [P, KT, T], f32r, 0)
    act_lo = at("act_lo", [P, KT, T], f32r, 32)
    X = at("X", [P, TT, D], f32, 64)
    ident = at("ident", [P, P], f32, 96)
    row_max = at("row_max", [P, 2], f32, 96.5)
    row_sum = at("row_sum", [P, 2], f32, 96.5625)
    sum_sq = at("sum_sq", [P, 2], f32, 96.625)
    var = at("var", [P, 2], f32, 96.6875)
    std = at("std", [P, 2], f32, 96.75)
    rstd0 = at("rstd0", [P, 2], f32, 96.8125)
    newt = at("newt", [P, 2, 2], f32, 96.875)
    rstd = at("rstd", [P, 2], f32, 96.9375)
    x_max = at("x_max", [P, 3, X_HEADS], f32, 97)
    x_neg = at("x_neg", [P, 3, X_HEADS], f32, 97.0625)
    x_sum = at("x_sum", [P, 3, X_HEADS], f32, 97.125)
    x_inv = at("x_inv", [P, 3, X_HEADS], f32, 97.1875)
    b_col = at("b_col", [8, 1], f32, 97.25)
    row_inv = at("row_inv", [P, 2], f32, 97.3125)
    slot_kb = [98, 106, 114, 134, 142, 150, 158, 166]
    w_hi = [at(f"w_hi{i}", [P, 1024], f32r, kb) for i, kb in enumerate(slot_kb)]
    w_lo = [at(f"w_lo{i}", [P, 1024], f32r, kb + 4) for i, kb in enumerate(slot_kb)]
    raw = [at(f"raw{i}", [P, 1024], f32, 122 + 4 * i) for i in range(2)]
    sets = [[134 + 32 * a + 16 * h for h in range(2)] for a in range(2)]
    qhl = [[at(f"qhl{a}{h}", [P, T], f32r, sets[a][h]) for h in range(2)] for a in range(2)]
    khh = [[at(f"khh{a}{h}", [P, T], f32r, sets[a][h] + 4) for h in range(2)] for a in range(2)]
    qb_ = [[at(f"qb{a}{h}", [HEAD + 4, T], f32r, sets[a][h] + 8) for h in range(2)] for a in range(2)]
    klb = [[at(f"klb{a}{h}", [HEAD + 4, T], f32r, sets[a][h] + 12) for h in range(2)] for a in range(2)]
    V = [at(f"V{a}", [P, TT, P], f32, kb) for a, kb in enumerate((198, 118))]
    vT = at("vT", [P, T], f32, 114)
    S = at("S", [P, S_BLOCKS * P], f32, 202)
    pT = at("pT", [P, T], f32, 126)
    mask = at("mask", [P, T], f32, 130)
    first_k = (at("first_k_hi", [P, 1024], f32r, 118), at("first_k_lo", [P, 1024], f32r, 126))
    raw_first = [at(f"raw_first{i}", [P, 1024], f32, 198 + 4 * i) for i in range(2)]
    gate_raw = at("gate_raw", [P, 1024], f32, 178)
    gate_hi = at("gate_hi", [P, 1024], f32r, 182)
    gate_lo = at("gate_lo", [P, 1024], f32r, 186)
    gate_z = at("gate_z", [8, T], f32, 190)
    gate_e = at("gate_e", [8, T], f32, 194)
    cum = at("cum", [8, T], f32, 202)
    cum_hi = at("cum_hi", [8, T], f32r, 166)
    cum_lo = at("cum_lo", [8, T], f32r, 170)
    a_hn = [at(f"a_hn{i}", [P, D], f32, 166 + 4 * i) for i in range(2)]
    a_gain = at("a_gain", [P, D], f32, 174)
    c_hn = [at(f"c_hn{i}", [P, D], f32, 174 + 4 * i) for i in range(2)]
    c_gain = at("c_gain", [P, D], f32, 182)
    x_hn = [at(f"x_hn{i}", [P, D], f32, kb) for i, kb in enumerate((186, 202))]
    x_gain = at("x_gain", [P, D], f32, 198)
    m_gain = at("m_gain", [P, D], f32, 186)
    m_in = at("m_in", [P, D], f32, 130)
    mT_hi = at("mT_hi", [P, KT, N_MEM], f32r, 190)
    mT_lo = at("mT_lo", [P, KT, N_MEM], f32r, 198)
    kx = at("kx", [P, KT, N_MEM], f32, 150)
    vx = at("vx", [P, MT, D], f32, 98)
    vxT = at("vxT", [P, 2, N_MEM], f32, 130)
    qx = at("qx", [P, KT, T], f32, 158)
    Sx = [at(f"Sx{i}", [P, X_HEADS, N_MEM], f32, kb) for i, kb in enumerate((106, 110, 130))]
    pTx = [at(f"pTx{i}", [P, 2 * X_HEADS, 2 * P], f32, 190 + 8 * i) for i in range(2)]
    r_ff = at("r_ff", [P, 2, HALF], f32, 130)
    a_hi = at("a_hi", [P, 4, T], f32r, 174)
    a_lo = at("a_lo", [P, 4, T], f32r, 190)
    f_hn = [at(f"f_hn{i}", [P, D], f32, 106 + 4 * i) for i in range(2)]
    f_gain = at("f_gain", [P, D], f32, 114)

    with ExitStack() as ctx:
        def sem(name):
            return ctx.enter_context(nc.semaphore(name))

        psS = [ctx.enter_context(nc.psum_tensor(f"psS{i}", [P, 1024], f32)) for i in range(2)]
        psG = [ctx.enter_context(nc.psum_tensor(f"psG{i}", [P, HALF], f32)) for i in range(2)]
        psO = ctx.enter_context(nc.psum_tensor("psO", [P, 2, HALF], f32))

        psX = [psS[0][:], psS[1][:], psO[:].rearrange("p a n -> p (a n)")]

        consts_loaded = sem("consts_loaded")
        b_loaded = sem("b_loaded")
        bias_stored = sem("bias_stored")
        gain_loaded = [sem(f"gain_loaded{i}") for i in range(5)]
        x_loaded = [sem(f"x_loaded{i}") for i in range(TT)]
        x_rest = [sem(f"x_rest{i}") for i in range(2)]
        m_loaded = [sem(f"m_loaded{i}") for i in range(MT)]
        rawB = sem("rawB_loaded")
        raw_first_loaded = [sem(f"raw_first_loaded{i}") for i in range(2)]
        rawC = [sem(f"rawC_loaded{i}") for i in range(2)]
        gate_zeroed = sem("gate_zeroed")
        gate_loaded = sem("gate_loaded")
        gate_hi_done = sem("gate_hi_done")
        gate_lo_done = sem("gate_lo_done")
        gate_act = sem("gate_act")
        gate_dve = sem("gate_dve")
        cum_stored = sem("cum_stored")
        bias_loaded = [sem(f"bias_loaded{i}") for i in range(2)]
        mask_loaded = sem("mask_loaded")
        hi_done = sem("hi_done")
        lo_done = sem("lo_done")
        tile_done = sem("tile_done")
        tile_out = sem("tile_out")
        qk_done = sem("qk_done")
        vt_done = sem("vt_done")
        vt_out = sem("vt_out")
        qk_hi = sem("qk_hi")
        raw_gate = sem("raw_gate")
        max_gate = sem("max_gate")
        max_done = sem("max_done")
        exp_done = sem("exp_done")
        inv_done = sem("inv_done")
        tr_done = sem("tr_done")
        pT_done = sem("pT_done")
        pv_done = sem("pv_done")
        o_out = sem("o_out")
        yt_done = sem("yt_done")
        y_hi = sem("y_hi")
        y_lo = sem("y_lo")
        n_sq = sem("n_sq")
        n_var = sem("n_var")
        n_std = sem("n_std")
        n_chain = sem("n_chain")
        n_hn = sem("n_hn")
        n_tr = sem("n_tr")
        n_hi = sem("n_hi")
        n_lo = sem("n_lo")
        sx_done = sem("sx_done")
        sx_max = sem("sx_max")
        sx_neg = sem("sx_neg")
        sx_exp = sem("sx_exp")
        sx_inv = sem("sx_inv")
        sx_norm = sem("sx_norm")
        sx_tr = sem("sx_tr")
        sx_pT = sem("sx_pT")
        hi_out = sem("hi_out")
        relu_out = sem("relu_out")
        sq_out = sem("sq_out")
        out_stored = [sem(f"out_stored{i}") for i in range(2)]

        PRO_TILES = len(FIRST_TILES)
        B_TILES = PRO_TILES + 7 * len(PAIR_TILES)
        def S_of(u):
            n = KEY_BLOCKS[u % STEPS]
            first = 0 if u % 2 == 0 else S_BLOCKS - n
            return S[:, first * P:(first + n) * P]

        QK_COUNT = {j: n + 1 for n, j in enumerate(j for j, (chunk, _) in enumerate(PAIR_TILES) if chunk != V_)}
        LAST = len(PAIR_TILES) - 1
        SPLIT_AT = {("T", 2): 1, ("PV", 6): 2, ("PV", 13): 3}
        B_BLOCKS = 3 * PAIRS

        def body_tile(p, j):
            return p * len(PAIR_TILES) + (PRO_TILES + j + 1)

        def pair_slot(par, chunk):
            return (3 * (1 - par) + chunk) % 2

        OUT_SLOTS = (3, 4, 5, 6, 0, 1, 2, 7)
        XO_SLOTS = (3, 4, 2, 1, 0, 5, 6, 7)
        X_SLOTS = (3, 4)
        MLP_SLOTS = XO_SLOTS

        LAST_COL = (PAIRS - 1) * P
        Y_PARTS = 2 * TT + 2

        OUT_STEPS = (1, 4, 7, 10)

        def raw_of(m):
            if m < 8:
                i = (0, 0, 0, 0, 1, 0, 1, 0)[m]
                return i, (1, 2, 3, 4, 1, 5, 2, 6)[m]
            return m % 2, m // 2 + (3 if m % 2 == 0 else -1)

        N_M, N_C, N_X, N_F = TT, TT + MT, 2 * TT + MT, 3 * TT + MT
        C_OUT, C_XK, C_XV, C_XQ, C_XO, C_MLP = 0, 8, 16, 24, 32, 40
        G_OUT = B_TILES
        G_XK = G_OUT + 2 * TT
        G_XV = G_XK + KT
        G_XQ = G_XV + 2 * KT
        G_PV = G_XQ + 2 * KT
        G_XO = G_PV + 2 * KT
        G_MLP = G_XO + 2 * TT
        MLP_TILES = 8 + 2 * TT

        def y_part(e):
            if e < 2 * TT:
                t, part = divmod(e, 2)
                n = 4 - part
                return psG[part][:, 0:n * P].rearrange("p (k t) -> p k t", t=P), slice(4 * part, 4 * part + n), slice(t * P, (t + 1) * P)
            i = e - 2 * TT
            return psS[i][:, 0:HALF], PAIRS - 1, slice(i * HALF, (i + 1) * HALF)

        block = ctx.enter_context(nc.Block())

        def pair_cols(w, p, j):
            c = (p // 4) * 3 * HALF + {V_: 2, Q_: 0, K_: 1}[j] * HALF + (p % 4) * P
            return w[:, :, c:c + P]

        @block.sync
        def _(sp):
            def gain(i, dst, g):
                sp.dma_start(dst[:], g.rearrange("(a d) -> a d", a=1).to_broadcast([P, D])).then_inc(gain_loaded[i], 16)

            def raw_pair(p, j, col=None):
                src = w_in_k[:, :, bass.ds(col, P)] if col is not None else pair_cols(w_in_k, p, j)
                if not isinstance(p, int) or 3 * p + j:
                    sp.wait_ge(lo_done, p * 3 + j)
                    sp.sem_inc(raw_gate, 1)
                sp.dma_start(raw[0][:].rearrange("p (k n) -> p k n", n=P), src).then_inc(rawB, 16)

            def bias(heads, par):
                for h, head in enumerate(heads):
                    for side, dst in ((0, qb_), (1, klb)):
                        rows4 = bias_rows[bass.ds(head, 1), 4 * side:4 * side + 4, :].rearrange("o r n -> (o r) n")
                        sp.dma_start(dst[par][h][HEAD:HEAD + 4, :].bitcast(f32), rows4).then_inc(bias_loaded[par], 16)

            def raw_block(m, i, src, shape):
                sp.wait_ge(lo_done, m + (B_BLOCKS - 1))
                sp.dma_start(shape(raw[i]), src).then_inc(rawC[i], 16)

            for t in range(TT):
                if t == 1:
                    gain(0, a_gain, g_mix)
                    sp.dma_start(ident[:], ident_c).then_inc(consts_loaded, 16)
                sp.dma_start(X[:, t, :], x_t[t]).then_inc(x_loaded[t], 16)
                if t == 3:
                    raw_pair(0, 0)
            for i in range(2):
                sp.dma_start(raw_first[i][:].rearrange("p (k n) -> p k n", n=P), pair_cols(w_in_k, 0, i + 1)).then_inc(raw_first_loaded[i], 16)
            sp.dma_start(b_col[:], b_forget.rearrange("(h a) -> h a", a=1)).then_inc(b_loaded, 16)
            sp.wait_ge(gate_zeroed, 1)
            sp.dma_start(gate_raw[:].rearrange("p (k n) -> p k n", n=P)[:, :, 0:8],
                         w_in_k[:, :, GATE_COL:GATE_COL + 8]).then_inc(gate_loaded, 16)
            sp.dma_start(bias_rows, bias_c).then_inc(bias_stored, 16)
            sp.dma_start(mask[:], masks_c[0]).then_inc(mask_loaded, 16)
            sp.wait_ge(bias_stored, 16)
            bias((0, 1), 0)
            for j in range(2):
                raw_pair(1, j)
            sp.wait_ge(gate_dve, 7)
            for r, src in ((4, cum_hi[:].bitcast(f32)), (5, cum_lo[:].bitcast(f32)), (2, gate_z[:]), (3, gate_e[:])):
                sp.dma_start(bias_rows[PAIRS:2 * PAIRS, r, :], src).then_inc(cum_stored, 16)
            sp.wait_ge(cum_stored, 64)

            def pair_loads(it, p, par):
                static = isinstance(p, int)
                k_col, next_col = (None, None) if static else (
                    sp.snap(((p + 1) // 4) * 1024 + (p + 1) * P + HALF), sp.snap(((p + 2) // 4) * 1024 + (p + 2) * P))
                heads = [2 * p + 2 + h if static else sp.snap(p * 2 + 2 + h) for h in range(2)]
                v_col = None if static else sp.snap(next_col + 2 * HALF)
                turn = None if static else sp.snap(it + 1)
                sp.wait_ge(qk_done, p * 16 + 1)
                bias(heads, 1 - par)
                raw_pair(p + 1, K_, k_col)
                if not static:
                    raw_pair(p + 2, V_, v_col)
                    raw_pair(p + 2, Q_, ((p + 2) // 4) * 1024 + (p + 2) * P)
                    if par == 1:
                        sp.wait_ge(max_done, p * 16 + 16)
                        sp.dma_start(mask[:], masks_c[bass.ds(turn, 1), :, :].rearrange("o p n -> (o p) n")).then_inc(mask_loaded, 16)

            with sp.Fori(0, 3) as it:
                for par in range(2):
                    pair_loads(it, it * 2 + par, par)
            pair_loads(3, 6, 0)
            def two_rows(w, half, i):
                return w[:, 2 * i:2 * i + 2, half * HALF:(half + 1) * HALF]

            def rows(r):
                return r[:].rearrange("p (k n) -> p k n", n=HALF)

            def cols(r):
                return r[:].rearrange("p (k n) -> p k n", n=P)

            def out_block(m):
                if m == 4:
                    sp.wait_ge(pv_done, PAIRS * STEPS)
                else:
                    before = max([n for n in range(m) if raw_of(n)[0] == raw_of(m)[0]], default=-1)
                    sp.wait_ge(lo_done, B_BLOCKS + before + 1)
                sp.dma_start(rows(raw[raw_of(m)[0]]), two_rows(w_out_k, m // 4, m % 4)).then_inc(rawC[raw_of(m)[0]], 16)

            out_block(0)
            for t in range(TT):
                sp.wait_ge(yt_done, 2 * t + 2)
                sp.dma_start(X[:, t, 0:LAST_COL], x_t[t][:, 0:LAST_COL]).then_inc(x_loaded[t], 16)
                if t in (1, 4, 6):
                    out_block({1: 1, 4: 2, 6: 3}[t])
            out_block(5)
            out_block(4)
            for i in range(2):
                sp.wait_ge(yt_done, 2 * TT + i + 1)
                for t in range(4 * i, 4 * i + 4):
                    sp.dma_start(X[:, t, LAST_COL:D], x_t[t][:, LAST_COL:D]).then_inc(x_rest[i], 16)
            gain(2, m_gain, g_mem)
            sp.dma_start(m_in[:], mem_t[0]).then_inc(m_loaded[0], 16)
            out_block(6)
            out_block(7)
            gain(1, c_gain, g_xattn)
            sp.wait_ge(n_hn, N_M + 1)
            sp.dma_start(m_in[:], mem_t[1]).then_inc(m_loaded[1], 16)
            for first, w in ((C_XK, w_xk_k), (C_XV, w_xv_k), (C_XQ, w_xq_k)):
                with sp.Fori(0, 4) as c:
                    for i in range(2):
                        raw_block(c * 2 + (first + i), i, w[:, :, bass.ds(c * 256 + i * P, P)], cols)
            for m in range(8):
                raw_block(C_XO + m, m % 2, two_rows(w_xo_k, m // 4, m % 4), rows)
                if m == 5:
                    sp.wait_ge(tile_done, G_XO)
                    gain(3, x_gain, g_mlp)
            with sp.Fori(0, GROUPS) as g:
                for i in range(8):
                    if i < 4:
                        raw_block(g * 8 + (C_MLP + i), i % 2, w_up_k[:, :, bass.ds(g * HALF + i * P, P)], cols)
                    else:
                        raw_block(g * 8 + (C_MLP + i), i % 2, w_down[bass.ds(g * HALF + (i - 4) * P, P), :], lambda r: r[:])
            sp.wait_ge(tile_done, G_MLP + (GROUPS - 1) * MLP_TILES + 8)
            gain(4, f_gain, g_final)
            for t in range(TT):
                sp.wait_ge(n_hn, N_F + t + 1)
                sp.dma_start(out_t[t], f_hn[t % 2][:]).then_inc(out_stored[t % 2], 16)
            for i in range(2):
                sp.wait_ge(out_stored[i], 16 * TT // 2)

        @block.tensor
        def _(pe):
            def split_products(dst, parts, last_inc=None):
                n = len(parts)
                for k, (sh, sl, mh, ml) in enumerate(parts):
                    nc.tensor.matmul(dst, sh, mh, start=(k == 0), stop=False)
                    nc.tensor.matmul(dst, sh, ml, start=False, stop=False)
                    mm = nc.tensor.matmul(dst, sl, mh, start=False, stop=(k == n - 1))
                return mm

            def col_block(slot_hi, slot_lo, k):
                return slot_hi[:, k * P:(k + 1) * P], slot_lo[:, k * P:(k + 1) * P]

            def proj(j, chunk, half, r0, r1, slots):
                for r in range(r0, r1):
                    k, part = divmod(r, 3)
                    hi, lo = col_block(*slots[chunk], k)
                    mh = act_hi[:, k, half * HALF:(half + 1) * HALF]
                    ml = act_lo[:, k, half * HALF:(half + 1) * HALF]
                    a, b = ((hi, mh), (hi, ml), (lo, mh))[part]
                    mm = nc.tensor.matmul(psG[j % 2][:], a, b, start=(r == 0), stop=(r == 23))
                    if r == 23:
                        mm.then_inc(tile_done, 1)

            def scores(par, h, qb, u):
                n = (qb + 1) * P
                rows_q = slice(qb * P, (qb + 1) * P)
                for c in range(0, n, HALF):
                    dst = psS[u % 2][:, c:min(n, c + HALF)]
                    keys = slice(c, min(n, c + HALF))
                    nc.tensor.matmul(dst, qhl[par][h][:, rows_q], khh[par][h][:, keys], start=True, stop=False)
                    mm = nc.tensor.matmul(dst, qb_[par][h][:, rows_q], klb[par][h][:, keys], start=False, stop=True)
                mm.then_inc(qk_done, 1)

            def v_transposes(i, region):
                for b in range(4):
                    c = (4 * i + b) * P
                    mm = nc.tensor.transpose(psS[region][:, HALF + b * P:HALF + (b + 1) * P], vT[:, c:c + P], ident[:])
                mm.then_inc(vt_done, 1)

            def norm_tr(n, src):
                pe.wait_ge(n_hn, n + 1)
                if n >= 2:
                    pe.wait_ge(n_lo, n - 1)
                for k in range(KT):
                    mm = nc.tensor.transpose(psS[n % 2][:, k * P:(k + 1) * P], src[:, k * P:(k + 1) * P], ident[:])
                mm.then_inc(n_tr, 1)

            pe.wait_ge(consts_loaded, 16)
            for t in range(TT // 2):
                norm_tr(t, a_hn[t % 2])
            slots = [(w_hi[0], w_lo[0]), (w_hi[1], w_lo[1]), first_k, (gate_hi, gate_lo)]
            for j, (chunk, half) in enumerate(FIRST_TILES):
                if j == 0:
                    pe.wait_ge(n_lo, TT // 2)
                if j == 4:
                    pe.wait_ge(n_lo, TT)
                if j < 3:
                    pe.wait_ge(lo_done, j + 1)
                if j == 3:
                    pe.wait_ge(gate_lo_done, 1)
                if j >= 2:
                    pe.wait_ge(tile_out, j - 1)
                proj(j, chunk, half, 0, PRODUCTS, slots)
                if j < 2:
                    norm_tr(TT // 2 + 2 * j, a_hn[0])
                    norm_tr(TT // 2 + 2 * j + 1, a_hn[1])
            for i in range(2):
                v_transposes(i, i)
            pe.wait_ge(bias_loaded[0], 64)
            pe.wait_ge(tile_out, PRO_TILES - 1)
            scores(0, 0, 0, 0)

            def out_product(t, r):
                k, part = divmod(r, 3)
                tok, cs = slice(t * P, (t + 1) * P), slice((k % 2) * HALF, (k % 2 + 1) * HALF)
                hi, lo = w_hi[OUT_SLOTS[k // 2]][:, cs], w_lo[OUT_SLOTS[k // 2]][:, cs]
                a, b = ((act_hi, hi), (act_hi, lo), (act_lo, hi))[part]
                return nc.tensor.matmul(psG[t % 2][:], a[:, k, tok], b, start=(r == 0), stop=(r == PRODUCTS - 1))

            def early_products(t, r0, r1):
                for r in range(r0, r1):
                    if r == 0:
                        pe.wait_ge(y_lo, 2 * TT - 1 + t)
                    if t == 0 and r % 6 == 0:
                        pe.wait_ge(lo_done, B_BLOCKS + C_OUT + r // 6 + 1)
                    out_product(t, r)

            def pair_pe(p, par, has_next):
                for ev in pair_steps(has_next):
                    kind, u = ev[0], ev[1]
                    h, qb = STEP[u % STEPS]
                    if kind == "T":
                        pe.wait_ge(exp_done, p * 16 + (u + 1))
                        for b in range(qb + 1):
                            mm = nc.tensor.transpose(psS[u % 2][:, b * P:(b + 1) * P], S_of(u)[:, b * P:(b + 1) * P], ident[:])
                        mm.then_inc(tr_done, 1)
                    elif kind == "QK":
                        if u >= 2:
                            pe.wait_ge(pT_done, p * 16 + (u - 1))
                        if u == STEPS:
                            pe.wait_ge(tile_out, body_tile(p, 3))
                            pe.wait_ge(bias_loaded[1 - par], bias_count(p, par))
                            scores(1 - par, 0, 0, u)
                        else:
                            if u == 3:
                                pe.wait_ge(tile_out, body_tile(p, -1))
                                pe.wait_ge(vt_out, p * 2 + 2)
                            elif u == 14 and has_next:
                                pe.wait_ge(vt_out, p * 2 + 4)
                            scores(par, h, qb, u)
                    elif kind == "Y":
                        t, part = divmod(u, 2)
                        if u == 0:
                            pe.wait_ge(o_out, p * 16)
                            pe.wait_ge(tile_out, body_tile(p, -1))
                        if u >= 2:
                            pe.wait_ge(y_lo, u - 1)
                        for b in range(4 - part):
                            k = 4 * part + b
                            mm = nc.tensor.transpose(psG[part][:, b * P:(b + 1) * P], X[:, t, k * P:(k + 1) * P], ident[:])
                        mm.then_inc(yt_done, 1)
                    elif kind == "P":
                        early_products(*ev[1:])
                    elif kind == "VT":
                        if u == 0:
                            pe.wait_ge(tile_out, body_tile(p, 1))
                        else:
                            pe.wait_ge(vt_out, p * 2 + 3)
                        v_transposes(u, 0)
                    elif kind == "G":
                        j, r0, r1 = ev[1:]
                        chunk, half = PAIR_TILES[j]
                        if r0 == 0:
                            pe.wait_ge(tile_out, body_tile(p, j - 2))
                            if half == 0:
                                pe.wait_ge(lo_done, p * 3 + (3 + chunk + 1))
                        slot = pair_slot(par, chunk)
                        proj(j, 0, half, r0, r1, [(w_hi[slot], w_lo[slot])])
                    elif kind == "PV":
                        if u == 0:
                            pe.wait_ge(vt_out, p * 2 + 2)
                        pe.wait_ge(pT_done, p * 16 + (u + 1))
                        if u >= 2:
                            pe.wait_ge(o_out, p * 16 + (u - 1))
                        for b in range(qb + 1):
                            mm = nc.tensor.matmul(psO[:, u % 2, 0:HEAD], pT[:, b * P:(b + 1) * P],
                                                  V[par][:, b, h * HEAD:(h + 1) * HEAD], start=(b == 0), stop=(b == qb))
                        mm.then_inc(pv_done, 1)

            def bias_count(p, par):
                if isinstance(p, int):
                    return 64 * ((p + 1) // 2 + 1)
                return (p + (2 + par)) * 32

            with pe.Fori(0, 3) as it:
                for par in range(2):
                    pair_pe(it * 2 + par, par, True)
            pair_pe(6, 0, True)
            pair_pe(7, 1, False)

            def token_tile(psum, t, slots4):
                parts = []
                for k in range(KT):
                    i = slots4[k // 2]
                    cs = slice((k % 2) * HALF, (k % 2 + 1) * HALF)
                    tok = slice(t * P, (t + 1) * P)
                    parts.append((act_hi[:, k, tok], act_lo[:, k, tok], w_hi[i][:, cs], w_lo[i][:, cs]))
                return split_products(psum[:], parts)

            def residual_product(g0, block0, w_slots, n0, hn, halves, before):
                for half in halves:
                    for t in range(TT):
                        g = g0 + half * TT + t
                        before(half, t)
                        if t == 0:
                            pe.wait_ge(lo_done, B_BLOCKS + block0 + 4 * half + 4)
                        pe.wait_ge(tile_out, g - 1)
                        token_tile(psG[g % 2], t, w_slots[4 * half:4 * half + 4]).then_inc(tile_done, 1)
                        if half and t >= 2:
                            norm_tr(n0 + t - 2, hn[(n0 + t) % 2])

            def last_y_transposes(i):
                pe.wait_ge(o_out, PAIRS * STEPS - (3, 0)[i])
                pe.wait_ge(pT_done, PAIRS * STEPS - 1 + i)
                for b in range(4):
                    mm = nc.tensor.transpose(psS[i][:, b * P:(b + 1) * P], X[:, 4 * i + b, LAST_COL:D], ident[:])
                mm.then_inc(yt_done, 1)

            last_y_transposes(0)
            early_products(1, EARLY_PRODUCTS - Y_PRODUCTS, Y_PRODUCTS)
            last_y_transposes(1)
            for t in range(TT):
                if t == 0:
                    pe.wait_ge(y_lo, 2 * TT + 1)
                if t == TT // 2:
                    pe.wait_ge(y_lo, Y_PARTS)
                if t >= 2:
                    pe.wait_ge(tile_out, G_OUT + t - 1)
                for r in range(Y_PRODUCTS if t < 2 else 0, PRODUCTS):
                    mm = out_product(t, r)
                mm.then_inc(tile_done, 1)

            def before_out(half, t):
                if t == 1:
                    for i in range(MT):
                        norm_tr(N_M + i, c_hn[i])

            def last_norm_trs(n0, hn):
                for t in (TT - 2, TT - 1):
                    norm_tr(n0 + t, hn[(n0 + t) % 2])

            residual_product(G_OUT, C_OUT, OUT_SLOTS, N_C, c_hn, (1,), before_out)

            def mem_chunk(g, slot):
                return split_products(psG[g % 2][:, 0:N_MEM],
                                      [(*col_block(w_hi[slot], w_lo[slot], k), mT_hi[:, k, :], mT_lo[:, k, :]) for k in range(KT)])

            pe.wait_ge(n_lo, N_M + MT)
            with pe.Fori(0, 4) as c:
                for i in range(2):
                    pe.wait_ge(lo_done, c * 2 + (B_BLOCKS + C_XK + i + 1))
                    pe.wait_ge(tile_out, c * 2 + (G_XK + i - 1))
                    mem_chunk(G_XK + i, X_SLOTS[i]).then_inc(tile_done, 1)
            last_norm_trs(N_C, c_hn)

            def xv_step(c, i, last):
                if not last:
                    pe.wait_ge(lo_done, c * 2 + (B_BLOCKS + C_XV + i + 2))
                    if not (isinstance(c, int) and c == 0 and i == 0):
                        pe.wait_ge(tile_out, c * 4 + (G_XV + 2 * i - 1))
                    mem_chunk(1 - i, X_SLOTS[1 - i]).then_inc(tile_done, 1)
                pe.wait_ge(tile_out, c * 4 + (G_XV + 2 * i + 1))
                for b in range(MT):
                    mm = nc.tensor.transpose(psO[:, i, b * P:(b + 1) * P], vxT[:, i, b * P:(b + 1) * P], ident[:])
                mm.then_inc(tile_done, 1)

            pe.wait_ge(lo_done, B_BLOCKS + C_XV + 1)
            pe.wait_ge(tile_out, G_XV)
            mem_chunk(0, X_SLOTS[0]).then_inc(tile_done, 1)
            with pe.Fori(0, 3) as c:
                for i in range(2):
                    xv_step(c, i, False)
            xv_step(3, 0, False)
            xv_step(3, 1, True)

            pe.wait_ge(n_lo, N_C + TT)
            def q_tile(i, half, bank):
                tok = slice(half * HALF, (half + 1) * HALF)
                split_products(psG[bank][:], [(*col_block(w_hi[X_SLOTS[i]], w_lo[X_SLOTS[i]], k), act_hi[:, k, tok], act_lo[:, k, tok])
                                              for k in range(KT)]).then_inc(tile_done, 1)

            with pe.Fori(0, 3) as c:
                for i in range(2):
                    pe.wait_ge(lo_done, c * 2 + (B_BLOCKS + C_XQ + i + 1))
                    for half in range(2):
                        pe.wait_ge(tile_out, c * 4 + (G_XQ + 2 * i + half - 1))
                        q_tile(i, half, half)
            for n, (i, half) in enumerate(Q_LAST[:3]):
                pe.wait_ge(lo_done, B_BLOCKS + C_XQ + 7 + i)
                pe.wait_ge(tile_out, G_XQ + 11 + n)
                q_tile(i, half, n % 2)

            def x_scores(t):
                if t == 0:
                    pe.wait_ge(tile_out, G_XQ + 14)
                if t == TT // 2:
                    pe.wait_ge(tile_out, G_PV)
                if t >= 3:
                    pe.wait_ge(sx_pT, t - 2)
                for h in range(X_HEADS):
                    for c in range(2):
                        mm = nc.tensor.matmul(psX[t % 3][:, h * N_MEM:(h + 1) * N_MEM], qx[:, 2 * h + c, t * P:(t + 1) * P],
                                              kx[:, 2 * h + c, :], start=(c == 0), stop=(c == 1))
                mm.then_inc(sx_done, 1)

            def x_transposes(t):
                pe.wait_ge(sx_norm, t + 1)
                for b in range(2 * X_HEADS):
                    h, c = divmod(b, 2)
                    mm = nc.tensor.transpose(psX[t % 3][:, b * P:(b + 1) * P], Sx[t % 3][:, h, c * P:(c + 1) * P], ident[:])
                mm.then_inc(sx_tr, 1)

            def x_outputs(q, part):
                pe.wait_ge(sx_pT, 2 * q + 2)
                for h in (2 * part, 2 * part + 1):
                    g = G_PV + X_HEADS * q + h
                    pe.wait_ge(tile_out, g - 1)
                    for jj in range(2):
                        j = 2 * h + jj
                        for c in range(MT):
                            mm = nc.tensor.matmul(psG[g % 2][:, jj * 256:(jj + 1) * 256], vx[:, c, j * P:(j + 1) * P],
                                                  pTx[q % 2][:, 2 * h + c, :], start=(c == 0), stop=(c == MT - 1))
                    mm.then_inc(tile_done, 1)

            for ev in X_STEPS:
                if ev[0] == "S":
                    x_scores(ev[1])
                elif ev[0] == "T":
                    x_transposes(ev[1])
                elif ev[0] == "O":
                    x_outputs(*ev[1:])
                elif ev[0] == "Q":
                    pe.wait_ge(tile_out, G_XQ + 14)
                    q_tile(1, 1, 1)

            residual_product(G_XO, C_XO, XO_SLOTS, N_X, x_hn, (0, 1), lambda half, t: None)

            def mlp_group(g):
                for j in range(8):
                    half, c = divmod(j, 4)
                    first = isinstance(g, int)
                    if half == 0:
                        pe.wait_ge(lo_done, g * 8 + (B_BLOCKS + C_MLP + c + 1))
                    if first and c == 0:
                        pe.wait_ge(n_lo, N_X + (half + 1) * TT // 2)
                    pe.wait_ge(tile_out, g * MLP_TILES + (G_MLP + j - 1))
                    tok = slice(half * HALF, (half + 1) * HALF)
                    split_products(psG[j % 2][:], [(*col_block(w_hi[MLP_SLOTS[c]], w_lo[MLP_SLOTS[c]], k), act_hi[:, k, tok], act_lo[:, k, tok])
                                                   for k in range(KT)]).then_inc(tile_done, 1)
                    if first and j == 1:
                        last_norm_trs(N_X, x_hn)
                for t in range(TT):
                    for half in range(2):
                        j = 8 + 2 * t + half
                        cs = slice(half * HALF, (half + 1) * HALF)
                        if t == 0 and half == 0:
                            pe.wait_ge(lo_done, g * 8 + (B_BLOCKS + C_MLP + 8))
                        pe.wait_ge(tile_out, g * MLP_TILES + (G_MLP + j - 1))
                        tok = slice(t * P, (t + 1) * P)
                        split_products(psG[half][:], [(a_hi[:, c, tok], a_lo[:, c, tok], w_hi[MLP_SLOTS[4 + c]][:, cs], w_lo[MLP_SLOTS[4 + c]][:, cs])
                                                      for c in range(4)]).then_inc(tile_done, 1)

            mlp_group(0)
            with pe.Fori(1, GROUPS) as g:
                mlp_group(g)

        @block.scalar
        def _(act):
            def split_hi(dst, src, sem_, *waits):
                for s_, v in waits:
                    act.wait_ge(s_, v)
                nc.scalar.activation(dst, src, ACT.Copy).then_inc(sem_, 1)

            def sq(n, src, *waits):
                for s_, v in waits:
                    act.wait_ge(s_, v)
                if n:
                    act.wait_ge(n_sq, n)
                nc.scalar.activation(psO[:].rearrange("p a n -> p (a n)"), src, ACT.Square, accum_out=sum_sq[:, n % 2:n % 2 + 1]).then_inc(n_sq, 1)

            def root(n):
                i = slice(n % 2, n % 2 + 1)
                act.wait_ge(n_var, n + 1)
                nc.scalar.activation(std[:, i], var[:, i], ACT.Sqrt).then_inc(n_std, 1)

            def norm_hi(n, dst):
                act.wait_ge(n_tr, n + 1)
                nc.scalar.activation(dst, psS[n % 2][:].rearrange("p (k t) -> p k t", t=P), ACT.Copy).then_inc(n_hi, 1)

            def act_tile(t):
                return act_hi[:, :, t * P:(t + 1) * P]

            for t in range(TT + 2):
                if t < TT:
                    sq(t, X[:, t, :], (x_loaded[t], 16))
                    root(t)
                if t >= 2:
                    norm_hi(t - 2, act_tile(t - 2))
                if t == 4:
                    split_hi(w_hi[0][:], raw[0][:], hi_done, (rawB, 16))
                if t in (5, 6):
                    i = t - 5
                    split_hi((w_hi[1], first_k[0])[i][:], raw_first[i][:], hi_done, (raw_first_loaded[i], 16))
            split_hi(gate_hi[:], gate_raw[:], gate_hi_done, (gate_loaded, 16))

            def qk_hi_out(j, chunk, half, a):
                tok = slice(half * HALF, (half + 1) * HALF)
                for h in range(2):
                    src = psG[j % 2][h * HEAD:(h + 1) * HEAD, :]
                    places = (qhl[a][h][0:HEAD, tok], qb_[a][h][0:HEAD, tok]) if chunk == Q_ else \
                             (khh[a][h][0:HEAD, tok], khh[a][h][HEAD:P, tok])
                    for dst in places:
                        e = nc.scalar.activation(dst, src, ACT.Copy, scale=1.0 / math.sqrt(HEAD) if chunk == Q_ else 1.0)
                e.then_inc(qk_hi, 1)

            for j, (chunk, half) in enumerate(FIRST_TILES):
                if chunk in (Q_, K_) and j < PRO_TILES - 1:
                    act.wait_ge(tile_done, j + 1)
                    qk_hi_out(j, chunk, half, 0)
                if chunk == V_ and half == 1:
                    act.wait_ge(tile_out, 5)
                    nc.scalar.activation(gate_e[:], gate_z[:], ACT.Abs).then_inc(gate_act, 1)
                    act.wait_ge(gate_act, 1)
                    nc.scalar.activation(gate_e[:], gate_e[:], ACT.Exp, scale=-1.0).then_inc(gate_act, 1)
                    act.wait_ge(gate_act, 2)
                    nc.scalar.activation(gate_e[:], gate_e[:], ACT.Ln, bias=1.0).then_inc(gate_act, 1)
                if chunk == Q_ and half == 1:
                    split_hi(w_hi[1][:], raw[0][:], hi_done, (rawB, 32))

            def exp_step(u, value):
                act.wait_ge(max_done, value)
                nc.scalar.activation(S_of(u), S_of(u), ACT.Exp, bias=row_max[:, u % 2:u % 2 + 1], scale=-1.0,
                                     accum_out=row_sum[:, u % 2:u % 2 + 1]).then_inc(exp_done, 1)

            exp_step(0, 1)

            act.wait_ge(cum_stored, 64)

            def block_hi(m, slot, value=None, i=None):
                if m is not None:
                    i, n = raw_of(m)
                    value = 16 * n
                act.wait_ge(rawC[i], value)
                nc.scalar.activation(w_hi[slot][:], raw[i][:], ACT.Copy).then_inc(hi_done, 1)

            def y_hi_out(e):
                act.wait_ge(yt_done, e + 1)
                src, k, tok = y_part(e)
                nc.scalar.activation(act_hi[:, k, tok], src, ACT.Copy).then_inc(y_hi, 1)

            def pair_act(p, par, has_next, splits):
                for ev in pair_steps(has_next):
                    kind, u = ev[0], ev[1]
                    if kind == "T":
                        n = KEY_BLOCKS[u] * P
                        act.wait_ge(tr_done, p * 16 + (u + 1))
                        nc.scalar.activation(pT[:, 0:n], psS[u % 2][:, 0:n], ACT.Copy).then_inc(pT_done, 1)
                        if u + 1 < STEPS or has_next:
                            exp_step(u + 1, p * 16 + (u + 2))
                        if not has_next and u in OUT_STEPS:
                            m = OUT_STEPS.index(u)
                            block_hi(C_OUT + m, OUT_SLOTS[m])
                    elif kind == "Y":
                        y_hi_out(u)
                    elif kind == "last":
                        act.wait_ge(tile_done, body_tile(p, -1))
                        qk_hi_out(LAST, *PAIR_TILES[LAST], par)
                    elif kind == "tile" and PAIR_TILES[u][0] != V_ and u != LAST:
                        act.wait_ge(tile_done, body_tile(p, u))
                        qk_hi_out(u, *PAIR_TILES[u], 1 - par)
                    ahead = SPLIT_AT.get((kind, u))
                    if ahead and has_next and (splits or ahead < 3):
                        act.wait_ge(tile_done, body_tile(p, {1: -1, 2: 1, 3: 4}[ahead]))
                        split_hi(w_hi[pair_slot(par, ahead)][:], raw[0][:], hi_done, (rawB, p * 48 + 16 * (ahead + 2)))

            with act.Fori(0, 3) as it:
                for par in range(2):
                    pair_act(it * 2 + par, par, True, True)
            pair_act(6, 0, True, False)
            pair_act(7, 1, False, False)
            for e in (2 * TT, 2 * TT + 1):
                y_hi_out(e)
            for m in range(4, 8):
                block_hi(C_OUT + m, OUT_SLOTS[m])
            sq(N_M, m_in[:], (m_loaded[0], 16))
            root(N_M)
            sq(N_M + 1, m_in[:], (m_loaded[1], 16))
            root(N_M + 1)
            for t in range(MT):
                norm_hi(N_M + t, mT_hi[:, :, t * P:(t + 1) * P])

            def residual_norm_act(g0, n0, extra, tiles=TT):
                for t in range(TT):
                    n = n0 + t
                    if t < tiles:
                        sq(n, X[:, t, :], (tile_out, g0 + TT + t + 1))
                        root(n)
                    if t >= 2:
                        norm_hi(n - 2, act_tile(t - 2))
                    extra(t)

            def last_norm_his(n0):
                for t in (TT - 2, TT - 1):
                    norm_hi(n0 + t, act_tile(t))

            def extra_c(t):
                if t in (2, 3):
                    block_hi(C_XK + t - 2, X_SLOTS[t - 2])

            residual_norm_act(G_OUT, N_C, extra_c, TT - 1)

            def xk_his(c):
                for i in range(2):
                    act.wait_ge(tile_done, c * 2 + (G_XK + i + 1))
                    block_hi(None, X_SLOTS[i], c * 16 + 16 * raw_of(C_XK + 2 + i)[1], i)

            xk_his(0)
            sq(N_C + TT - 1, X[:, TT - 1, :], (tile_out, G_OUT + 2 * TT))
            root(N_C + TT - 1)
            with act.Fori(1, 4) as c:
                xk_his(c)
            last_norm_his(N_C)
            with act.Fori(0, 4) as c:
                for i in range(2):
                    act.wait_ge(tile_done, c * 4 + (G_XV + 2 * i + 1))
                    block_hi(None, X_SLOTS[i], c * 16 + 16 * raw_of(C_XV + 2 + i)[1], i)
            with act.Fori(0, 3) as c:
                for i in range(2):
                    act.wait_ge(tile_done, c * 4 + (G_XQ + 2 * i + 2))
                    block_hi(None, X_SLOTS[i], c * 16 + 16 * raw_of(C_XQ + 2 + i)[1], i)
            act.wait_ge(tile_done, G_XQ + 15)
            block_hi(C_XO, XO_SLOTS[0])

            def x_exp(t):
                act.wait_ge(sx_neg, t + 1)
                for h in range(X_HEADS):
                    e = nc.scalar.activation(Sx[t % 3][:, h, :], psX[t % 3][:, h * N_MEM:(h + 1) * N_MEM], ACT.Exp,
                                             bias=x_neg[:, t % 3, h:h + 1], accum_out=x_sum[:, t % 3, h:h + 1])
                e.then_inc(sx_exp, 1)

            def x_pT(t):
                q = t // 2
                if t % 2 == 0 and q >= 2:
                    act.wait_ge(tile_done, G_PV + X_HEADS * (q - 1))
                act.wait_ge(sx_tr, t + 1)
                o = (t % 2) * P
                nc.scalar.activation(pTx[q % 2][:, :, o:o + P], psX[t % 3].rearrange("p (b t) -> p b t", t=P), ACT.Copy).then_inc(sx_pT, 1)

            def x_out(q, part):
                for h in (2 * part, 2 * part + 1):
                    g = G_PV + X_HEADS * q + h
                    act.wait_ge(tile_done, g + 1)
                    nc.scalar.activation(act_hi[:, 2 * h:2 * h + 2, q * 256:(q + 1) * 256],
                                         psG[g % 2][:].rearrange("p (j t) -> p j t", j=2), ACT.Copy).then_inc(hi_out, 1)

            for ev in X_STEPS:
                if ev[0] == "S":
                    x_exp(ev[1])
                elif ev[0] == "T":
                    x_pT(ev[1])
                elif ev[0] == "O":
                    x_out(*ev[1:])
                elif ev[0] == "Q":
                    act.wait_ge(tile_done, G_XQ + 16)
                    block_hi(C_XO + 1, XO_SLOTS[1])
                    block_hi(C_XO + 2, XO_SLOTS[2])
                if ev == ("O", 2, 1):
                    block_hi(C_XO + 3, XO_SLOTS[3])
            for m in range(4, 8):
                if m == 4:
                    act.wait_ge(tile_done, G_XO)
                block_hi(C_XO + m, XO_SLOTS[m])

            def extra_x(t):
                if t in (1, 2, 3, 4):
                    block_hi(C_MLP + t - 1, MLP_SLOTS[t - 1])
            residual_norm_act(G_XO, N_X, extra_x)
            def mlp_group(g, first, last):
                for j in range(8):
                    half, c = divmod(j, 4)
                    act.wait_ge(tile_done, g * MLP_TILES + (G_MLP + j + 1))
                    act.wait_ge(tile_out, g * MLP_TILES + (G_MLP + j - 1))
                    nc.scalar.activation(r_ff[:, j % 2, :], psG[j % 2][:], ACT.Relu).then_inc(relu_out, 1)
                    act.wait_ge(sq_out, g * 8 + (j + 1))
                    nc.scalar.activation(a_hi[:, c, half * HALF:(half + 1) * HALF], r_ff[:, j % 2, :], ACT.Copy).then_inc(hi_out, 1)
                    if first and j == 1:
                        last_norm_his(N_X)
                    if first and 2 <= j < 6:
                        block_hi(C_MLP + 2 + j, MLP_SLOTS[2 + j])
                    if half == 0 and not first:
                        block_hi(None, MLP_SLOTS[4 + c], g * 64 + 16 * raw_of(C_MLP + 4 + c)[1], c % 2)
                    if half == 1 and not last and not first:
                        block_hi(None, MLP_SLOTS[c], g * 64 + 16 * raw_of(C_MLP + 8 + c)[1], c % 2)
                if first:
                    for c in range(4):
                        block_hi(C_MLP + 8 + c, MLP_SLOTS[c])

            mlp_group(0, True, False)
            with act.Fori(1, GROUPS - 1) as g:
                mlp_group(g, False, False)
            mlp_group(GROUPS - 1, False, True)
            for t in range(TT):
                n = N_F + t
                sq(n, X[:, t, :], (tile_out, G_MLP + (GROUPS - 1) * MLP_TILES + 8 + 2 * t + 2))
                root(n)

        @block.vector
        def _(dve):
            def lo_part(dst, src, hi, sem_):
                nc.vector.tensor_tensor(dst, src, hi.bitcast(f32), ALU.subtract).then_inc(sem_, 1)

            def norm_var(n):
                i = slice(n % 2, n % 2 + 1)
                dve.wait_ge(n_sq, n + 1)
                nc.vector.tensor_scalar(var[:, i], sum_sq[:, i], 1.0 / D, EPS, ALU.mult, ALU.add).then_inc(n_var, 1)

            def norm_scale(n, src, dst, gain_t, *waits):
                i = slice(n % 2, n % 2 + 1)
                dve.wait_ge(n_std, n + 1)
                nc.vector.reciprocal(rstd0[:, i], std[:, i]).then_inc(n_chain, 1)
                dve.wait_ge(n_chain, 4 * n + 1)
                nc.vector.scalar_tensor_tensor(newt[:, 0, i], rstd0[:, i], rstd0[:, i], var[:, i], ALU.mult, ALU.mult).then_inc(n_chain, 1)
                dve.wait_ge(n_chain, 4 * n + 2)
                nc.vector.tensor_scalar(newt[:, 1, i], newt[:, 0, i], -0.5, 1.5, ALU.mult, ALU.add).then_inc(n_chain, 1)
                dve.wait_ge(n_chain, 4 * n + 3)
                nc.vector.tensor_tensor(rstd[:, i], rstd0[:, i], newt[:, 1, i], ALU.mult).then_inc(n_chain, 1)
                dve.wait_ge(n_chain, 4 * n + 4)
                for s_, v in waits:
                    dve.wait_ge(s_, v)
                nc.vector.scalar_tensor_tensor(dst[:], src, rstd[:, i], gain_t[:], ALU.mult, ALU.mult).then_inc(n_hn, 1)

            def norm_lo(n, dst_lo, dst_hi):
                dve.wait_ge(n_hi, n + 1)
                lo_part(dst_lo, psS[n % 2][:].rearrange("p (k t) -> p k t", t=P), dst_hi, n_lo)

            def act_tile(a, t):
                return a[:, :, t * P:(t + 1) * P]

            def block_lo(n, slot, src, places=None):
                dve.wait_ge(hi_done, n + 1)
                hi, lo = places or (w_hi[slot], w_lo[slot])
                lo_part(lo[:], src[:], hi[:], lo_done)

            def later_lo(m, slot):
                block_lo(B_BLOCKS + m, slot, raw[raw_of(m)[0]])

            def tile_rest(j, chunk, half, a, hi_count):
                tok = slice(half * HALF, (half + 1) * HALF)
                if chunk == V_:
                    nc.vector.tensor_copy(vT[:, tok], psG[j % 2][:]).then_inc(tile_out, 1)
                else:
                    dve.wait_ge(qk_hi, hi_count)
                    for h in range(2):
                        src = psG[j % 2][h * HEAD:(h + 1) * HEAD, :]
                        if chunk == Q_:
                            e = nc.vector.scalar_tensor_tensor(qhl[a][h][HEAD:P, tok], src, 1.0 / math.sqrt(HEAD),
                                                               qhl[a][h][0:HEAD, tok].bitcast(f32), ALU.mult, ALU.subtract)
                        else:
                            e = nc.vector.tensor_tensor(klb[a][h][0:HEAD, tok], src, khh[a][h][0:HEAD, tok].bitcast(f32),
                                                        ALU.subtract)
                    e.then_inc(tile_out, 1)

            nc.vector.memset(gate_raw[:], 0.0).then_inc(gate_zeroed, 1)
            for t in range(TT + 2):
                if t < TT:
                    norm_var(t)
                if t == 0:
                    norm_scale(0, X[:, 0, :], a_hn[0], a_gain, (gain_loaded[0], 16))
                if 2 <= t <= TT:
                    if t >= 3:
                        dve.wait_ge(n_tr, t - 2)
                    norm_scale(t - 1, X[:, t - 1, :], a_hn[(t - 1) % 2], a_gain, (gain_loaded[0], 16))
                if t >= 2:
                    norm_lo(t - 2, act_tile(act_lo, t - 2), act_tile(act_hi, t - 2))
                if t in (4, 5, 6):
                    i = t - 4
                    block_lo(i, i, (raw[0], *raw_first)[i], first_k if i == 2 else None)
                if t == TT:
                    dve.wait_ge(tile_done, 1)
                    tile_rest(0, *FIRST_TILES[0], 0, None)
            dve.wait_ge(gate_hi_done, 1)
            lo_part(gate_lo[:], gate_raw[:], gate_hi[:], gate_lo_done)

            def v_out(i, a, region):
                nc.vector.tensor_copy(V[a][:, 4 * i:4 * i + 4, :],
                                      psS[region][:, HALF:2 * HALF].rearrange("p (b d) -> p b d", d=P)).then_inc(vt_out, 1)

            dve.wait_ge(b_loaded, 16)
            for j, (chunk, half) in enumerate(FIRST_TILES):
                if j == 0:
                    continue
                if j == PRO_TILES - 1:
                    break
                dve.wait_ge(tile_done, j + 1)
                if chunk == GATE_:
                    nc.vector.tensor_scalar(gate_z[:, half * HALF:(half + 1) * HALF], psG[j % 2][0:8, :], b_col[:], None,
                                            ALU.add).then_inc(tile_out, 1)
                else:
                    tile_rest(j, chunk, half, 0, {1: 1, 2: 2, 6: 3, 7: 4}.get(j))
                if j == 6:
                    block_lo(3, 1, raw[0])
                if j == 5:
                    dve.wait_ge(gate_act, 1)
                    nc.vector.tensor_scalar(gate_z[:], gate_z[:], -1.0, 0.0, ALU.mult, ALU.max).then_inc(gate_dve, 1)
                    dve.wait_ge(gate_dve, 1)
                    dve.wait_ge(gate_act, 3)
                    nc.vector.tensor_tensor(gate_z[:], gate_z[:], gate_e[:], ALU.add).then_inc(gate_dve, 1)
                    dve.wait_ge(gate_dve, 2)
                    nc.vector.tensor_tensor_scan(cum[:], gate_z[:], gate_z[:], 0.0, ALU.add, ALU.bypass).then_inc(gate_dve, 1)
                    dve.wait_ge(gate_dve, 3)
                    nc.vector.tensor_copy(cum_hi[:], cum[:]).then_inc(gate_dve, 1)
                    dve.wait_ge(gate_dve, 4)
                    nc.vector.tensor_tensor(cum_lo[:], cum[:], cum_hi[:].bitcast(f32), ALU.subtract).then_inc(gate_dve, 1)
                    dve.wait_ge(gate_dve, 5)
                    nc.vector.tensor_scalar(gate_z[:], cum_hi[:].bitcast(f32), -1.0, None, ALU.mult).then_inc(gate_dve, 1)
                    nc.vector.tensor_scalar(gate_e[:], cum_lo[:].bitcast(f32), -1.0, None, ALU.mult).then_inc(gate_dve, 1)

            def max_step(u, value):
                n = KEY_BLOCKS[u % STEPS] * P
                dve.wait_ge(qk_done, value)
                dve.sem_inc(max_gate, 1)
                nc.vector.tensor_tensor_reduce(out=S_of(u), in0=psS[u % 2][:, 0:n], in1=mask[:, T - n:T], scale=-1.0,
                                               scalar=3.0e38, op0=ALU.add, op1=ALU.min,
                                               accum_out=row_max[:, u % 2:u % 2 + 1]).then_inc(max_done, 1)

            for i in range(2):
                dve.wait_ge(vt_done, i + 1)
                v_out(i, 0, i)
            dve.wait_ge(mask_loaded, 16)
            max_step(0, 1)
            dve.wait_ge(cum_stored, 64)

            def y_split(e):
                dve.wait_ge(y_hi, e + 1)
                src, k, tok = y_part(e)
                lo_part(act_lo[:, k, tok], src, act_hi[:, k, tok], y_lo)

            def pair_dve(it, p, par, has_next, splits):
                for ev in pair_steps(has_next):
                    kind, u = ev[0], ev[1]
                    h, qb = STEP[u % STEPS]
                    if kind == "QK":
                        if u == STEPS and splits and par == 1:
                            dve.wait_ge(mask_loaded, it * 16 + 32)
                        max_step(u, p * 16 + (u + 1))
                    elif kind == "PV":
                        i = slice(u % 2, u % 2 + 1)
                        dve.wait_ge(exp_done, p * 16 + (u + 1))
                        nc.vector.reciprocal(row_inv[:, i], row_sum[:, i]).then_inc(inv_done, 1)
                        dve.wait_ge(inv_done, p * 16 + (u + 1))
                        dve.wait_ge(pv_done, p * 16 + (u + 1))
                        dst = X[:, qb, bass.ds(p * P + h * HEAD, HEAD)]
                        nc.vector.tensor_scalar(dst, psO[:, u % 2, 0:HEAD], row_inv[:, i], None,
                                                ALU.mult).then_inc(o_out, 1)
                    elif kind == "tile":
                        chunk, half = PAIR_TILES[u]
                        dve.wait_ge(tile_done, body_tile(p, u))
                        if u != LAST:
                            tile_rest(u, chunk, half, 1 - par, p * 4 + (4 + QK_COUNT.get(u, 0)))
                    elif kind == "Y":
                        y_split(u)
                    elif kind == "last":
                        dve.wait_ge(tile_done, body_tile(p, -1))
                        tile_rest(LAST, *PAIR_TILES[LAST], par, p * 4 + 4)
                    elif kind == "VT":
                        dve.wait_ge(vt_done, p * 2 + (u + 3))
                        v_out(u, 1 - par, 0)
                    elif kind == "T" and not has_next and u in OUT_STEPS:
                        m = OUT_STEPS.index(u)
                        later_lo(C_OUT + m, OUT_SLOTS[m])
                    ahead = SPLIT_AT.get((kind, u))
                    if ahead and has_next and (splits or ahead < 3):
                        block_lo(p * 3 + (3 + ahead), pair_slot(par, ahead), raw[0])

            with dve.Fori(0, 3) as it:
                for par in range(2):
                    pair_dve(it, it * 2 + par, par, True, True)
            pair_dve(3, 6, 0, True, False)
            pair_dve(3, 7, 1, False, False)

            def add_residual(g, t, half):
                dve.wait_ge(tile_done, g + 1)
                cs = slice(half * HALF, (half + 1) * HALF)
                nc.vector.tensor_tensor(X[:, t, cs], X[:, t, cs], psG[g % 2][:], ALU.add).then_inc(tile_out, 1)

            for e in (2 * TT, 2 * TT + 1):
                y_split(e)
            for t in range(1, TT):
                dve.wait_ge(x_loaded[t - 1], 32)
                add_residual(G_OUT + t - 1, t - 1, 0)
                if t in (2, 3, 4, 5):
                    later_lo(C_OUT + 2 + t, OUT_SLOTS[2 + t])
                if t == 6:
                    norm_var(N_M)
                    norm_scale(N_M, m_in[:], c_hn[0], m_gain, (gain_loaded[2], 16))
            dve.wait_ge(x_loaded[TT - 1], 32)
            add_residual(G_OUT + TT - 1, TT - 1, 0)
            norm_var(N_M + 1)
            norm_scale(N_M + 1, m_in[:], c_hn[1], m_gain, (gain_loaded[2], 16))
            for t in range(MT):
                norm_lo(N_M + t, mT_lo[:, :, t * P:(t + 1) * P], mT_hi[:, :, t * P:(t + 1) * P])

            def residual_norm_dve(g0, n0, hn, gain_t, gain_sem, extra, tiles=TT):
                for t in range(TT):
                    n = n0 + t
                    if g0 == G_OUT and t % 4 == 0:
                        dve.wait_ge(x_rest[t // 4], 64)
                    add_residual(g0 + TT + t, t, 1)
                    if t < tiles:
                        norm_var(n)
                    if t >= 2:
                        norm_lo(n - 2, act_tile(act_lo, t - 2), act_tile(act_hi, t - 2))
                    if t < tiles:
                        norm_scale(n, X[:, t, :], hn[n % 2], gain_t, (gain_sem, 16), (n_tr, n - 1))
                    extra(t)

            def last_norm_los(n0):
                for t in (TT - 2, TT - 1):
                    norm_lo(n0 + t, act_tile(act_lo, t), act_tile(act_hi, t))

            def extra_c(t):
                if t in (2, 3):
                    later_lo(C_XK + t - 2, X_SLOTS[t - 2])
            residual_norm_dve(G_OUT, N_C, c_hn, c_gain, gain_loaded[1], extra_c, TT - 1)

            def xk_out(c):
                for i in range(2):
                    dve.wait_ge(tile_done, c * 2 + (G_XK + i + 1))
                    nc.vector.tensor_copy(kx[:, bass.ds(c * 2 + i, 1), :].rearrange("p o n -> p (o n)"),
                                          psG[(G_XK + i) % 2][:, 0:N_MEM]).then_inc(tile_out, 1)
                    block_lo(c * 2 + (B_BLOCKS + C_XK + 2 + i), X_SLOTS[i], raw[i])

            xk_out(0)
            n = N_C + TT - 1
            norm_var(n)
            norm_scale(n, X[:, TT - 1, :], c_hn[n % 2], c_gain, (gain_loaded[1], 16), (n_tr, n - 1))
            with dve.Fori(1, 4) as c:
                xk_out(c)
            last_norm_los(N_C)
            def xv_out(c, i, last):
                block_lo(c * 2 + (B_BLOCKS + C_XV + 2 + i), X_SLOTS[i], raw[i])
                if not last:
                    dve.wait_ge(tile_done, c * 4 + (G_XV + 2 * i + 2))
                    nc.vector.tensor_copy(vxT[:, 1 - i, :], psG[1 - i][:, 0:N_MEM]).then_inc(tile_out, 1)
                dve.wait_ge(tile_done, c * 4 + (G_XV + 2 * i + (2 if last else 3)))
                nc.vector.tensor_copy(vx[:, :, bass.ds(c * 256 + i * P, P)],
                                      psO[:, i, 0:N_MEM].rearrange("p (b d) -> p b d", d=P)).then_inc(tile_out, 1)

            dve.wait_ge(tile_done, G_XV + 1)
            nc.vector.tensor_copy(vxT[:, 0, :], psG[0][:, 0:N_MEM]).then_inc(tile_out, 1)
            with dve.Fori(0, 3) as c:
                for i in range(2):
                    xv_out(c, i, False)
            xv_out(3, 0, False)
            xv_out(3, 1, True)
            def q_out(n, chunk, half, bank):
                dve.wait_ge(tile_done, n + (G_XQ + 1))
                nc.vector.tensor_scalar(qx[:, bass.ds(chunk, 1), half * HALF:(half + 1) * HALF].rearrange("p o n -> p (o n)"),
                                        psG[bank][:], 1.0 / math.sqrt(D // X_HEADS), None, ALU.mult).then_inc(tile_out, 1)

            with dve.Fori(0, 3) as c:
                for i in range(2):
                    for half in range(2):
                        q_out(c * 4 + (2 * i + half), c * 2 + i, half, half)
                    block_lo(c * 2 + (B_BLOCKS + C_XQ + 2 + i), X_SLOTS[i], raw[i])
            for n, (i, half) in enumerate(Q_LAST[:3]):
                q_out(12 + n, 6 + i, half, n % 2)
            later_lo(C_XO, XO_SLOTS[0])

            def x_row_max(t):
                dve.wait_ge(sx_done, t + 1)
                nc.vector.tensor_reduce(x_max[:, t % 3, :], psX[t % 3].rearrange("p (h n) -> p h n", n=N_MEM),
                                        AX.X, ALU.max).then_inc(sx_max, 1)
                dve.wait_ge(sx_max, t + 1)
                nc.vector.tensor_scalar(x_neg[:, t % 3, :], x_max[:, t % 3, :], -1.0, None, ALU.mult).then_inc(sx_neg, 1)

            def x_normalise(t):
                dve.wait_ge(sx_exp, t + 1)
                nc.vector.reciprocal(x_inv[:, t % 3, :], x_sum[:, t % 3, :]).then_inc(sx_inv, 1)
                dve.wait_ge(sx_inv, t + 1)
                nc.vector.tensor_tensor(Sx[t % 3][:], Sx[t % 3][:],
                                        x_inv[:, t % 3, :].rearrange("p (h o) -> p h o", o=1).to_broadcast([P, X_HEADS, N_MEM]),
                                        ALU.mult).then_inc(sx_norm, 1)

            def x_out_lo(q, part):
                for h in (2 * part, 2 * part + 1):
                    g = G_PV + X_HEADS * q + h
                    dve.wait_ge(hi_out, X_HEADS * q + h + 1)
                    tok = slice(q * 256, (q + 1) * 256)
                    lo_part(act_lo[:, 2 * h:2 * h + 2, tok], psG[g % 2][:].rearrange("p (j t) -> p j t", j=2),
                            act_hi[:, 2 * h:2 * h + 2, tok], tile_out)

            for ev in X_STEPS:
                if ev[0] == "S":
                    x_row_max(ev[1])
                elif ev[0] == "N":
                    x_normalise(ev[1])
                elif ev[0] == "O":
                    x_out_lo(*ev[1:])
                elif ev[0] == "Q":
                    q_out(15, 7, 1, 1)
                    later_lo(C_XO + 1, XO_SLOTS[1])
                    later_lo(C_XO + 2, XO_SLOTS[2])
                if ev == ("O", 2, 1):
                    later_lo(C_XO + 3, XO_SLOTS[3])
            for m in range(4, 8):
                later_lo(C_XO + m, XO_SLOTS[m])
            for t in range(TT):
                add_residual(G_XO + t, t, 0)

            def extra_x(t):
                if t in (1, 2, 3, 4):
                    later_lo(C_MLP + t - 1, MLP_SLOTS[t - 1])
            residual_norm_dve(G_XO, N_X, x_hn, x_gain, gain_loaded[3], extra_x)

            def mlp_group(g, first, last):
                for j in range(8):
                    half, c = divmod(j, 4)
                    cs = slice(half * HALF, (half + 1) * HALF)
                    dve.wait_ge(relu_out, g * 8 + (j + 1))
                    nc.vector.tensor_tensor(r_ff[:, j % 2, :], r_ff[:, j % 2, :], r_ff[:, j % 2, :], ALU.mult).then_inc(sq_out, 1)
                    dve.wait_ge(hi_out, g * 8 + (2 * KT + j + 1))
                    lo_part(a_lo[:, c, cs], r_ff[:, j % 2, :], a_hi[:, c, cs], tile_out)
                    if first and j == 1:
                        last_norm_los(N_X)
                    if first and 2 <= j < 6:
                        later_lo(C_MLP + 2 + j, MLP_SLOTS[2 + j])
                    if half == 0 and not first:
                        block_lo(g * 8 + (B_BLOCKS + C_MLP + 4 + c), MLP_SLOTS[4 + c], raw[c % 2])
                    if half == 1 and not last and not first:
                        block_lo(g * 8 + (B_BLOCKS + C_MLP + 8 + c), MLP_SLOTS[c], raw[c % 2])
                for t in range(TT):
                    for half in range(2):
                        dve.wait_ge(tile_done, g * MLP_TILES + (G_MLP + 8 + 2 * t + half + 1))
                        cs = slice(half * HALF, (half + 1) * HALF)
                        nc.vector.tensor_tensor(X[:, t, cs], X[:, t, cs], psG[half][:], ALU.add).then_inc(tile_out, 1)
                    if first and 1 <= t <= 4:
                        later_lo(C_MLP + 7 + t, MLP_SLOTS[t - 1])
                    if last:
                        final_norm(t)

            def final_norm(t):
                norm_var(N_F + t)
                if t:
                    final_scale(t - 1)

            def final_scale(t):
                n = N_F + t
                if t >= 2:
                    dve.wait_ge(out_stored[n % 2], 16 * (t // 2))
                norm_scale(n, X[:, t, :], f_hn[n % 2], f_gain, (gain_loaded[4], 16))

            mlp_group(0, True, False)
            with dve.Fori(1, GROUPS - 1) as g:
                mlp_group(g, False, False)
            mlp_group(GROUPS - 1, False, True)
            final_scale(TT - 1)


_INS = ["x", "mem", "g_mix", "w_in", "b_forget", "w_out", "g_xattn", "g_mem", "w_xq", "w_xk", "w_xv", "w_xo",
        "g_mlp", "w_up", "w_down", "g_final"]


def _shape_constants():
    ident = np.eye(P, dtype=np.float32)
    delta = (T - P) + np.arange(P)[:, None] - np.arange(T)[None, :]
    times = sum(((delta >= 0) & (delta <= w) & (delta % d == 0)).astype(np.int64) for w, d in DILATIONS)
    dilated = np.where(times > 0, np.log(np.maximum(times, 1)), NEG).astype(np.float32)
    causal = np.where(delta >= 0, 0.0, NEG).astype(np.float32)
    slopes = 2.0 ** -np.arange(1, 9, dtype=np.float64)
    bias = np.zeros((2 * PAIRS, 8, T), np.float32)
    bias[:, (0, 1, 6, 7), :] = 1.0
    alibi = (slopes[:, None] * np.arange(T)[None, :]).astype(np.float32)
    bias[:PAIRS, 2], bias[:PAIRS, 4] = -alibi, alibi
    return {"ident": ident, "masks": np.stack([dilated, dilated, causal, causal]), "bias": bias}


def kernel(**inputs):
    import concourse.bacc as _bacc
    from concourse.bass_utils import run_bass_kernel_spmd as _run

    nc = _bacc.Bacc("TRN2", target_bir_lowering=False, num_devices=1)
    arrays, args = {}, []
    for name in _INS:
        a = np.ascontiguousarray(inputs[name])
        arrays[f"in_{name}_dram"] = a
        args.append(nc.dram_tensor(f"in_{name}_dram", a.shape, mybir.dt.from_np(a.dtype), kind="ExternalInput").ap())
    for name, a in _shape_constants().items():
        arrays[f"const_{name}_dram"] = a
        args.append(nc.dram_tensor(f"const_{name}_dram", a.shape, mybir.dt.from_np(a.dtype), kind="ExternalInput").ap())
    args.append(nc.dram_tensor("out_0_dram", (1, T, D), mybir.dt.float32, kind="ExternalOutput").ap())
    hybrid_layer(nc, *args)
    r = _run(nc, [arrays], core_ids=[0])
    return r.results[0]["out_0_dram"]
```
